# Optimizing a Trainium2 kernel written in Bass

```python
import math
import jax, jax.numpy as jnp
from jax import lax
import numpy as np

D_MODEL = 1024
BATCH = 1
SEQ = 256
DEPTH = 2

CHUNK = 64
N_MIXERS = 3
ROPE_THETA = 500000.0
EPS = 1e-6
NEG = -1e30

SWA_HEADS = 16
SWA_KV_HEADS = 2
SWA_HEAD_DIM = 64
SWA_WINDOW = 128
SWA_WINDOW_CHUNKS = SWA_WINDOW // CHUNK
SWA_ROT_DIM = SWA_HEAD_DIM // 4
SWA_QKV_DIM = (SWA_HEADS + 2 * SWA_KV_HEADS) * SWA_HEAD_DIM

SSM_D_INNER = 2 * D_MODEL
SSM_HEAD_DIM = 64
SSM_HEADS = SSM_D_INNER // SSM_HEAD_DIM
SSM_GROUPS = 8
SSM_STATE = 128
SSM_CONV = 4
SSM_BLOCK = CHUNK
SSM_CONV_DIM = SSM_D_INNER + 2 * SSM_GROUPS * SSM_STATE
SSM_IN_DIM = SSM_D_INNER + SSM_CONV_DIM + SSM_HEADS

MLA_HEADS = 16
MLA_Q_RANK = 768
MLA_KV_RANK = 256
MLA_NOPE_DIM = 64
MLA_ROPE_DIM = 32
MLA_V_DIM = 64
MLA_Q_BLOCK = 128
MLA_DOWN_DIM = MLA_Q_RANK + MLA_KV_RANK + MLA_ROPE_DIM

D_FF = 3584
N_EXPERTS = 8
TOP_K = 2

kernel_name = 'hybrid_swa_ssd_mla_moe_trunk'

def rmsnorm(x, g):
    xf = x.astype(jnp.float32)
    y = xf * lax.rsqrt(jnp.mean(xf * xf, axis=-1, keepdims=True) + EPS)
    return (y * g.astype(jnp.float32)).astype(x.dtype)

def rope_tables(positions, rot_dim):
    inv_freq = ROPE_THETA ** (-jnp.arange(0, rot_dim, 2, dtype=jnp.float32) / rot_dim)
    ang = positions.astype(jnp.float32)[..., None] * inv_freq
    return jnp.cos(ang), jnp.sin(ang)

def _apply_rope(t, cos, sin):
    tf = t.astype(jnp.float32)
    t1, t2 = jnp.split(tf, 2, axis=-1)
    c = cos[:, :, None, :]
    s = sin[:, :, None, :]
    return jnp.concatenate([t1 * c - t2 * s, t2 * c + t1 * s], axis=-1).astype(t.dtype)

def _partial_rope(t, cos, sin):
    return jnp.concatenate([_apply_rope(t[..., :SWA_ROT_DIM], cos, sin), t[..., SWA_ROT_DIM:]], axis=-1)

def _band_chunks(t, n_back):
    n_chunks = t.shape[1]
    tp = jnp.pad(t, [(0, 0), (n_back, 0)] + [(0, 0)] * (t.ndim - 2))
    return jnp.concatenate([tp[:, j:j + n_chunks] for j in range(n_back + 1)], axis=2)

def swa_sink_attention(h, cos, sin, w_qkv, b_qkv, sinks, w_o):
    bsz, seq, _ = h.shape
    n_chunks = seq // CHUNK
    grp = SWA_HEADS // SWA_KV_HEADS
    n_back = SWA_WINDOW_CHUNKS - 1
    qkv = h @ w_qkv + b_qkv
    q, k, v = jnp.split(qkv, [SWA_HEADS * SWA_HEAD_DIM, (SWA_HEADS + SWA_KV_HEADS) * SWA_HEAD_DIM], axis=-1)
    q = _partial_rope(q.reshape(bsz, seq, SWA_HEADS, SWA_HEAD_DIM), cos, sin)
    k = _partial_rope(k.reshape(bsz, seq, SWA_KV_HEADS, SWA_HEAD_DIM), cos, sin)
    q = q.reshape(bsz, n_chunks, CHUNK, SWA_KV_HEADS, grp, SWA_HEAD_DIM)
    k = _band_chunks(k.reshape(bsz, n_chunks, CHUNK, SWA_KV_HEADS, SWA_HEAD_DIM), n_back)
    v = _band_chunks(v.reshape(bsz, n_chunks, CHUNK, SWA_KV_HEADS, SWA_HEAD_DIM), n_back)
    s = jnp.einsum('bcqkgd,bcskd->bckgqs', q, k, preferred_element_type=jnp.float32) * (SWA_HEAD_DIM ** -0.5)
    key_chunk = jnp.arange(n_chunks)[:, None] - n_back + jnp.arange(n_back + 1)[None, :]
    valid = jnp.repeat(key_chunk >= 0, CHUNK, axis=1)
    s = jnp.where(valid[None, :, None, None, None, :], s, NEG)
    sink = sinks.astype(jnp.float32).reshape(1, 1, SWA_KV_HEADS, grp, 1, 1)
    m = jnp.maximum(jnp.max(s, axis=-1, keepdims=True), sink)
    p = jnp.exp(s - m)
    p = p / (jnp.sum(p, axis=-1, keepdims=True) + jnp.exp(sink - m))
    o = jnp.einsum('bckgqs,bcskd->bcqkgd', p.astype(v.dtype), v)
    return o.reshape(bsz, seq, SWA_HEADS * SWA_HEAD_DIM) @ w_o

def _causal_dwconv(u, w, b):
    y = lax.conv_general_dilated(u, w[:, None, :].astype(u.dtype), window_strides=(1,), padding=[(SSM_CONV - 1, 0)], dimension_numbers=('NWC', 'WIO', 'NWC'), feature_group_count=u.shape[-1])
    return y + b

def _ssd_scan(x, dt, a, bm, cm):
    bsz, seq, grp, rep, hp = x.shape
    n_chunks = seq // SSM_BLOCK
    blk = SSM_BLOCK

    def to_chunks(t):
        return jnp.moveaxis(t.reshape(bsz, n_chunks, blk, *t.shape[2:]), 1, 0)

    causal = jnp.tril(jnp.ones((blk, blk), dtype=bool))

    def step(state, inp):
        xk, dtk, bk, ck = inp
        xf = xk.astype(jnp.float32)
        bf = bk.astype(jnp.float32)
        cf = ck.astype(jnp.float32)
        acum = jnp.cumsum(dtk * a, axis=1)
        seg = acum[:, :, None] - acum[:, None, :]
        decay = jnp.exp(jnp.where(causal[None, :, :, None, None], seg, -jnp.inf))
        cb = jnp.einsum('btgn,bsgn->btsg', cf, bf)
        xdt = xf * dtk[..., None]
        y_diag = jnp.einsum('btsgr,bsgrp->btgrp', cb[..., None] * decay, xdt)
        y_off = jnp.einsum('btgn,bgrpn->btgrp', cf, state) * jnp.exp(acum)[..., None]
        last = acum[:, -1]
        w_s = jnp.exp(last[:, None] - acum)
        new_state = state * jnp.exp(last)[..., None, None] + jnp.einsum('bsgn,bsgr,bsgrp->bgrpn', bf, w_s, xdt)
        return new_state, (y_diag + y_off).astype(xk.dtype)

    state0 = jnp.zeros((bsz, grp, rep, hp, bm.shape[-1]), jnp.float32)
    _, y = lax.scan(step, state0, (to_chunks(x), to_chunks(dt), to_chunks(bm), to_chunks(cm)))
    return jnp.moveaxis(y, 0, 1).reshape(x.shape)

def mamba2_ssd(h, w_in, conv_w, conv_b, dt_bias, a_log, d_skip, norm_g, w_out):
    bsz, seq, _ = h.shape
    rep = SSM_HEADS // SSM_GROUPS
    zxbcdt = h @ w_in
    z, xbc, dt = jnp.split(zxbcdt, [SSM_D_INNER, SSM_D_INNER + SSM_CONV_DIM], axis=-1)
    xbc = jax.nn.silu(_causal_dwconv(xbc, conv_w, conv_b))
    xs, bm, cm = jnp.split(xbc, [SSM_D_INNER, SSM_D_INNER + SSM_GROUPS * SSM_STATE], axis=-1)
    xs = xs.reshape(bsz, seq, SSM_GROUPS, rep, SSM_HEAD_DIM)
    bm = bm.reshape(bsz, seq, SSM_GROUPS, SSM_STATE)
    cm = cm.reshape(bsz, seq, SSM_GROUPS, SSM_STATE)
    dt = jax.nn.softplus(dt.astype(jnp.float32) + dt_bias.astype(jnp.float32)).reshape(bsz, seq, SSM_GROUPS, rep)
    a = -jnp.exp(a_log.astype(jnp.float32)).reshape(SSM_GROUPS, rep)
    y = _ssd_scan(xs, dt, a, bm, cm)
    y = y + xs * d_skip.reshape(SSM_GROUPS, rep)[..., None].astype(xs.dtype)
    y = y.reshape(bsz, seq, SSM_D_INNER)
    y = rmsnorm(y * jax.nn.silu(z), norm_g)
    return y @ w_out

def mla_attention(h, cos, sin, w_down, q_norm, kv_norm, w_uq, w_ukv, w_o):
    bsz, seq, _ = h.shape
    lat = h @ w_down
    c_q, c_kv, k_rope = jnp.split(lat, [MLA_Q_RANK, MLA_Q_RANK + MLA_KV_RANK], axis=-1)
    q = (rmsnorm(c_q, q_norm) @ w_uq).reshape(bsz, seq, MLA_HEADS, MLA_NOPE_DIM + MLA_ROPE_DIM)
    q_nope, q_rope = jnp.split(q, [MLA_NOPE_DIM], axis=-1)
    q_rope = _apply_rope(q_rope, cos, sin)
    kv = (rmsnorm(c_kv, kv_norm) @ w_ukv).reshape(bsz, seq, MLA_HEADS, MLA_NOPE_DIM + MLA_V_DIM)
    k_nope, v = jnp.split(kv, [MLA_NOPE_DIM], axis=-1)
    k_rope = _apply_rope(k_rope[:, :, None, :], cos, sin)[:, :, 0, :]
    scale = (MLA_NOPE_DIM + MLA_ROPE_DIM) ** -0.5
    n_blocks = seq // MLA_Q_BLOCK
    key_chunk = jnp.arange(seq) // CHUNK

    def to_blocks(t):
        return jnp.moveaxis(t.reshape(bsz, n_blocks, MLA_Q_BLOCK, *t.shape[2:]), 1, 0)

    def attend(args):
        qn, qr, idx = args
        q_chunk = (idx * MLA_Q_BLOCK + jnp.arange(MLA_Q_BLOCK)) // CHUNK
        s = (jnp.einsum('bqhd,bkhd->bhqk', qn, k_nope, preferred_element_type=jnp.float32) + jnp.einsum('bqhr,bkr->bhqk', qr, k_rope, preferred_element_type=jnp.float32)) * scale
        s = jnp.where(key_chunk[None, :] <= q_chunk[:, None], s, NEG)
        p = jax.nn.softmax(s, axis=-1)
        return jnp.einsum('bhqk,bkhd->bqhd', p.astype(v.dtype), v)

    o = lax.map(attend, (to_blocks(q_nope), to_blocks(q_rope), jnp.arange(n_blocks)))
    o = jnp.moveaxis(o, 0, 1).reshape(bsz, seq, MLA_HEADS * MLA_V_DIM)
    return o @ w_o

def swiglu(h, w_gu, w_down):
    g, u = jnp.split(h @ w_gu, 2, axis=-1)
    return (jax.nn.silu(g) * u) @ w_down

def moe_swiglu(h, w_router, w_gu, w_down):
    logits = (h @ w_router).astype(jnp.float32)
    top_v, top_i = lax.top_k(logits, TOP_K)
    gates = jax.nn.softmax(top_v, axis=-1)
    combine = jnp.sum(jax.nn.one_hot(top_i, N_EXPERTS, dtype=jnp.float32) * gates[..., None], axis=-2)
    combine = combine.astype(h.dtype)
    out = jnp.zeros_like(h)
    for e in range(N_EXPERTS):
        out = out + combine[..., e:e + 1] * swiglu(h, w_gu[e], w_down[e])
    return out

def setup_inputs(seed: int = 0) -> dict:
    key = jax.random.key(seed)
    ks = iter(jax.random.split(key, 48))

    def nrm(shape, fan_in):
        return jax.random.normal(next(ks), shape, jnp.float32) * (fan_in ** -0.5)

    def gain(shape):
        return 1.0 + 0.02 * jax.random.normal(next(ks), shape, jnp.float32)

    def small(shape, scale):
        return scale * jax.random.normal(next(ks), shape, jnp.float32)

    n_a = len(range(0, DEPTH, N_MIXERS))
    n_b = len(range(1, DEPTH, N_MIXERS))
    n_c = len(range(2, DEPTH, N_MIXERS))
    n_dense = len(range(0, DEPTH, 2))
    n_moe = len(range(1, DEPTH, 2))

    x = jax.random.normal(next(ks), (BATCH, SEQ, D_MODEL), jnp.float32)
    offset = jax.random.randint(next(ks), (BATCH, 1), 0, 1 << 16, dtype=jnp.int32)
    positions = offset + jnp.arange(SEQ, dtype=jnp.int32)[None, :]

    dt0 = jnp.exp(jax.random.uniform(next(ks), (n_b, SSM_HEADS), jnp.float32, minval=math.log(1e-3), maxval=math.log(1e-1)))
    ssm_dt_bias = dt0 + jnp.log(-jnp.expm1(-dt0))
    ssm_a_log = jnp.log(jax.random.uniform(next(ks), (n_b, SSM_HEADS), jnp.float32, minval=1.0, maxval=16.0))

    return {
        'x': x,
        'positions': positions,
        'ln_mix': gain((DEPTH, D_MODEL)),
        'ln_ffn': gain((DEPTH, D_MODEL)),
        'ln_final': gain((D_MODEL,)),
        'swa_w_qkv': nrm((n_a, D_MODEL, SWA_QKV_DIM), D_MODEL),
        'swa_b_qkv': small((n_a, SWA_QKV_DIM), 0.01),
        'swa_sinks': small((n_a, SWA_HEADS), 0.5),
        'swa_w_o': nrm((n_a, SWA_HEADS * SWA_HEAD_DIM, D_MODEL), SWA_HEADS * SWA_HEAD_DIM),
        'ssm_w_in': nrm((n_b, D_MODEL, SSM_IN_DIM), D_MODEL),
        'ssm_conv_w': nrm((n_b, SSM_CONV, SSM_CONV_DIM), SSM_CONV),
        'ssm_conv_b': small((n_b, SSM_CONV_DIM), 0.01),
        'ssm_dt_bias': ssm_dt_bias,
        'ssm_a_log': ssm_a_log,
        'ssm_d': gain((n_b, SSM_HEADS)),
        'ssm_norm': gain((n_b, SSM_D_INNER)),
        'ssm_w_out': nrm((n_b, SSM_D_INNER, D_MODEL), SSM_D_INNER),
        'mla_w_down': nrm((n_c, D_MODEL, MLA_DOWN_DIM), D_MODEL),
        'mla_q_norm': gain((n_c, MLA_Q_RANK)),
        'mla_kv_norm': gain((n_c, MLA_KV_RANK)),
        'mla_w_uq': nrm((n_c, MLA_Q_RANK, MLA_HEADS * (MLA_NOPE_DIM + MLA_ROPE_DIM)), MLA_Q_RANK),
        'mla_w_ukv': nrm((n_c, MLA_KV_RANK, MLA_HEADS * (MLA_NOPE_DIM + MLA_V_DIM)), MLA_KV_RANK),
        'mla_w_o': nrm((n_c, MLA_HEADS * MLA_V_DIM, D_MODEL), MLA_HEADS * MLA_V_DIM),
        'ffn_w_gu': nrm((n_dense, D_MODEL, 2 * D_FF), D_MODEL),
        'ffn_w_down': nrm((n_dense, D_FF, D_MODEL), D_FF),
        'moe_w_router': nrm((n_moe, D_MODEL, N_EXPERTS), D_MODEL),
        'moe_w_gu': nrm((n_moe, N_EXPERTS, D_MODEL, 2 * D_FF), D_MODEL),
        'moe_w_down': nrm((n_moe, N_EXPERTS, D_FF, D_MODEL), D_FF),
    }

def reference(x, positions, ln_mix, ln_ffn, ln_final, swa_w_qkv, swa_b_qkv, swa_sinks, swa_w_o, ssm_w_in, ssm_conv_w, ssm_conv_b, ssm_dt_bias, ssm_a_log, ssm_d, ssm_norm, ssm_w_out, mla_w_down, mla_q_norm, mla_kv_norm, mla_w_uq, mla_w_ukv, mla_w_o, ffn_w_gu, ffn_w_down, moe_w_router, moe_w_gu, moe_w_down):
    cos_a, sin_a = rope_tables(positions, SWA_ROT_DIM)
    cos_c, sin_c = rope_tables(positions, MLA_ROPE_DIM)
    h = x
    for i in range(DEPTH):
        hn = rmsnorm(h, ln_mix[i])
        kind, j = i % N_MIXERS, i // N_MIXERS
        if kind == 0:
            mix = swa_sink_attention(hn, cos_a, sin_a, swa_w_qkv[j], swa_b_qkv[j], swa_sinks[j], swa_w_o[j])
        elif kind == 1:
            mix = mamba2_ssd(hn, ssm_w_in[j], ssm_conv_w[j], ssm_conv_b[j], ssm_dt_bias[j], ssm_a_log[j], ssm_d[j], ssm_norm[j], ssm_w_out[j])
        else:
            mix = mla_attention(hn, cos_c, sin_c, mla_w_down[j], mla_q_norm[j], mla_kv_norm[j], mla_w_uq[j], mla_w_ukv[j], mla_w_o[j])
        h = h + mix
        hn = rmsnorm(h, ln_ffn[i])
        f = i // 2
        if i % 2 == 0:
            h = h + swiglu(hn, ffn_w_gu[f], ffn_w_down[f])
        else:
            h = h + moe_swiglu(hn, moe_w_router[f], moe_w_gu[f], moe_w_down[f])
    return rmsnorm(h, ln_final)


_drawn_inputs = setup_inputs


def setup_inputs(seed=0):
    import zlib

    import numpy as np

    out = dict(_drawn_inputs(seed))
    spreads = {}
    factors = {}
    for name, (base, spread) in spreads.items():
        noise = np.random.default_rng([zlib.crc32(name.encode()), seed]).standard_normal(out[name].shape)
        drawn = base * np.exp(spread * noise) if base else spread * noise
        out[name] = __import__('jax').numpy.asarray(drawn.astype(out[name].dtype))
    for name, factor in factors.items():
        out[name] = (out[name] * factor).astype(out[name].dtype)
    return out
```

```python
import math
from contextlib import ExitStack

import numpy as np
import concourse.bass as bass
from concourse import mybir

ALU = mybir.AluOpType
ACT = mybir.ActivationFunctionType
F32 = mybir.dt.float32
F32R = mybir.dt.float32r
I32 = mybir.dt.int32
AXX = mybir.AxisListType.X

P = 128
T = 256
TT = T // P
D = 1024
KD = D // P
EPS = 1e-6
CH = 64
HEADS, KV, HD = 16, 2, 64
PAIRS = HEADS // 2
QKV = (HEADS + 2 * KV) * HD
ROT = HD // 4
NF = ROT // 2
THETA = 500000.0
FF = 3584
KF = FF // P
NJ = FF // 512
DI = 2 * D
KI = DI // P
G, REP, N = 8, 4, 128
SH = G * REP
CONV = 4
CT = (DI + 2 * G * N) // P
E = 8

RING = 6
SPLIT = 3
AHEAD = 2
SLOT = 2048
LAYER_CHUNKS = 6 * NJ


def build(nc, x, positions, ln_mix, ln_ffn, ln_final, swa_w_qkv, swa_b_qkv, swa_sinks, swa_w_o,
          ssm_w_in, ssm_conv_w, ssm_conv_b, ssm_dt_bias, ssm_a_log, ssm_d, ssm_norm, ssm_w_out,
          ffn_w_gu, ffn_w_down, moe_w_router, moe_w_gu, moe_w_down, out):
    ctx = ExitStack()

    def sb(name, shape, dt=F32):
        return ctx.enter_context(nc.sbuf_tensor(name, shape, dt))

    def sem(name):
        return ctx.enter_context(nc.semaphore(name))

    with ctx:
        def block_of(w, k0, k, a, n):
            return w.rearrange("(k p) n -> p k n", p=P)[:, k0:k0 + k, a:a + n]

        def halves(w, a, n):
            return [[(block_of(w, k0, 4, a, n), 4, 0, n)] for k0 in (0, 4)]

        B0, C0 = DI + DI, DI + DI + G * N
        stream = []
        for a, n in ((0, 512), (512, 512), (1024, 256)):
            stream += halves(swa_w_qkv[0], a, n)
        for a in (0, 512):
            stream += halves(swa_w_o[0], a, 512)
        for j in range(NJ):
            stream += halves(ffn_w_gu[0], j * 512, 512) + halves(ffn_w_gu[0], FF + j * 512, 512)
        for c in range(KF // 2):
            stream.append([(block_of(ffn_w_down[0], 2 * c, 2, 0, D), 2, 0, D)])
        for a in range(0, DI, 512):
            stream += halves(ssm_w_in[0], a, 512)
        for g in range(G):
            for k0 in (0, 4):
                stream.append([(block_of(ssm_w_in[0], k0, 4, DI + 256 * g, 256), 4, 0, 256),
                               (block_of(ssm_w_in[0], k0, 4, B0 + 128 * g, 128), 4, 256, 128),
                               (block_of(ssm_w_in[0], k0, 4, C0 + 128 * g, 128), 4, 384, 128)])
        for c in range(KI // 2):
            stream.append([(block_of(ssm_w_out[0], 2 * c, 2, 0, D), 2, 0, D)])
        QKV0, WO0, FGU0 = 0, 6, 10
        FDN0 = FGU0 + 4 * NJ
        Z0 = FDN0 + KF // 2
        GR0, SO0, MOE0 = Z0 + 8, Z0 + 8 + 2 * G, Z0 + 8 + 2 * G + KI // 2
        assert len(stream) == MOE0 and MOE0 % RING == 0 and LAYER_CHUNKS % RING == 0

        ring = sb("ring", [P, RING, SLOT])
        w_hi = sb("w_hi", [P, SPLIT, SLOT], F32R)
        w_lo = sb("w_lo", [P, SPLIT, SLOT], F32R)
        slot_loaded = [sem(f"slot_loaded{r}") for r in range(RING)]
        hi_ready = sem("hi_ready")
        lo_ready = sem("lo_ready")
        chunk_used = sem("chunk_used")

        def loads_until(n):
            return sum(16 * len(stream[m]) for m in range(n % RING, n + 1, RING))

        slot_base = [loads_until(MOE0 - RING + r) for r in range(RING)]

        def chunk(n, w):
            return tuple(v[:, n % SPLIT, 0:SLOT // w * w].rearrange("p (k n) -> p k n", n=w)
                         for v in (w_hi, w_lo))

        h = sb("h", [P, TT, D])
        xs = sb("xs", [P, TT, D])
        hT = sb("hT", [P, KD, T])
        hT_hi = sb("hT_hi", [P, KD, T], F32R)
        hT_lo = sb("hT_lo", [P, KD, T], F32R)
        ident = sb("ident", [P, P])
        tri = sb("tri", [P, P])
        tri_lt = sb("tri_lt", [P, P])
        ones = sb("ones", [P, P])
        places = sb("places", [P, P])
        jlt = sb("jlt", [P, E, E])
        xs_hi = hT_hi[:].rearrange("p k (a b) -> p (k a b)", a=TT).rearrange("p (t d) -> p t d", t=TT)
        xs_lo = hT_lo[:].rearrange("p k (a b) -> p (k a b)", a=TT).rearrange("p (t d) -> p t d", t=TT)
        invf = sb("invf", [P, NF])
        vT = sb("vT", [P, P])
        cwT = sb("cwT", [P, CONV, CT])
        sinks_in = sb("sinks_in", [P, HEADS])
        sinks = sb("sinks", [P, HEADS])
        dtb = sb("dtb", [P, SH])
        alog = sb("alog", [P, SH])
        dsk = sb("dsk", [P, SH])
        dtw = sb("dtw", [P, KD, SH])
        rw = sb("rw", [P, KD, E])
        pos_i = sb("pos_i", [P, TT], I32)
        st = sb("st", [P, 5, 8])
        trig = sb("trig", [P, 4, TT, 2 * NF])
        sm = sb("sm", [P, TT, 4, HEADS])
        dts = sb("dts", [P, 12, 2 * SH])
        rt = sb("rt", [P, 16, TT * E])
        flag = sb("flag", [P, 1])
        place17 = sb("place17", [P, TT, 2 * E + 1])
        gate17 = sb("gate17", [P, TT, 2 * E + 1])
        passes_i = sb("passes_i", [P, 1], I32)

        def phase(**shapes):
            with ExitStack() as held:
                return [held.enter_context(nc.sbuf_tensor(name, [P, *s[0]], s[1]))[:] for name, s in shapes.items()]

        qkv, kd, qT, kT, vmid, prob, pT, oT_hi = phase(
            qkv=((TT, QKV), F32), kd=((TT, KV, 2, HD), F32), qT=((PAIRS, T), F32), kT=((KV, T), F32),
            vmid=((KV * HD,), F32), prob=((TT, HEADS, P), F32), pT=((HEADS, P), F32),
            oT_hi=((PAIRS, T), F32R))
        oT_lo, = phase(oT_lo=((PAIRS, T), F32R))
        brow = prob[:].rearrange("p a b c -> p (a b c)")[:, 0:QKV]
        rtmp = pT[:].rearrange("p a b -> p (a b)")[:, 0:4 * (HEADS + KV) * NF]
        vecs = pT[:, 8]
        cwr = pT[:, 9]
        f_hT_hi, f_hT_lo = phase(f_hT_hi=((KF, T), F32R), f_hT_lo=((KF, T), F32R))
        f_sg, f_hh = xs[:, 0].rearrange("p (t n) -> p t n", t=TT), xs[:, 1].rearrange("p (t n) -> p t n", t=TT)
        z, y, U, acc, XC, Xdt, arg, M, CBm = phase(
            z=((TT, DI), F32), y=((TT, DI), F32), U=((4, T + 3), F32), acc=((4, T), F32), XC=((4, T), F32),
            Xdt=((TT, REP * 64), F32), arg=((3, REP, P), F32), M=((3, REP, P), F32), CBm=((3, P), F32))
        yT_hi, _, yT_lo, yT = phase(yT_hi=((KI, T), F32R), under=((TT, DI), F32), yT_lo=((KI, T), F32R),
                                    yT=((2, 512), F32))
        m_sg, m_hh, m_hT_hi, m_hT_lo, xgT_hi, xgT_lo, sel, gsel, gselT, yg, gfin, cmp8 = phase(
            m_sg=((1, 512), F32), m_hh=((1, 512), F32), m_hT_hi=((KF, P), F32R), m_hT_lo=((KF, P), F32R),
            xgT_hi=((KD, P), F32R), xgT_lo=((KD, P), F32R), sel=((TT, P), F32R), gsel=((TT, P), F32),
            gselT=((TT, P), F32), yg=((D,), F32), gfin=((D,), F32), cmp8=((2, TT, E * E), F32))

        bank = [ctx.enter_context(nc.psum_tensor(f"bank{i}", [P, 512], F32)) for i in range(8)]

        def place_of(head):
            return (head % 2) * PAIRS + head // 2

        x_loaded, pos_loaded, vec_loaded, bc_loaded, bias_loaded, dtw_loaded = map(
            sem, ("x_loaded", "pos_loaded", "vec_loaded", "bc_loaded", "bias_loaded", "dtw_loaded"))
        const_ready, vec_T, vec_sb = map(sem, ("const_ready", "vec_T", "vec_sb"))
        sq_done, var_done, sqrt_done, xs_done, xT_mm, hT_done, h_done = map(
            sem, ("sq_done", "var_done", "sqrt_done", "xs_done", "xT_mm", "hT_done", "h_done"))
        angle_done, trig_done, qkv_mm, qkv_sb, rope_done, qkT_mm, qkT_sb, s_mm, sm_sub, sm_exp = map(
            sem, ("angle_done", "trig_done", "qkv_mm", "qkv_sb", "rope_done", "qkT_mm", "qkT_sb", "s_mm",
                  "sm_sub", "sm_exp"))
        p_ready, pT_mm, pT_sb, o_mm, o_sb, wo_mm = map(
            sem, ("p_ready", "pT_mm", "pT_sb", "o_mm", "o_sb", "wo_mm"))
        f_gate, f_up, f_silu, f_h, f_T, f_Tsb = map(
            sem, ("f_gate", "f_up", "f_silu", "f_h", "f_T", "f_Tsb"))
        c_dt, c_nabs, c_e, c_u1, c_ln, c_ea, c_dtA, c_acol, c_z, c_zs = map(
            sem, ("c_dt", "c_nabs", "c_e", "c_u1", "c_ln", "c_ea", "c_dtA", "c_acol", "c_z", "c_zs"))
        c_proj, c_u, c_pad, c_conv, c_xc, c_xT, c_cb, c_abc, c_xd, c_arg, c_exp, c_m, c_y, c_yadd = map(
            sem, ("c_proj", "c_u", "c_pad", "c_conv", "c_xc", "c_xT", "c_cb", "c_abc", "c_xd", "c_arg",
                  "c_exp", "c_m", "c_y", "c_yadd"))
        c_gated, c_sq, c_var, c_sqrt, c_yn, c_yT, c_yTsb = map(
            sem, ("c_gated", "c_sq", "c_var", "c_sqrt", "c_yn", "c_yT", "c_yTsb"))
        r_logit, r_max, r_exp, r_sel, r_cnt, r_passes = map(
            sem, ("r_logit", "r_max", "r_exp", "r_sel", "r_cnt", "r_passes"))
        m_S, m_gath, m_xg, m_gs, m_gt, m_gtsb, m_silu, m_h, m_T, m_Tsb, m_y, m_ysb, m_comb, \
            m_add = map(sem, ("m_S", "m_gath", "m_xg", "m_gs", "m_gt", "m_gtsb", "m_silu",
                              "m_h", "m_T", "m_Tsb", "m_y", "m_ysb", "m_comb", "m_add"))
        out_ready, out_stored = map(sem, ("out_ready", "out_stored"))
        gain_loaded = sem("gain_loaded")
        xs_his, xs_los = map(sem, ("xs_his", "xs_los"))
        hT_his, hT_los, o_los, f_This, c_yTg, c_yThi, m_This, m_xghi = map(
            sem, ("hT_his", "hT_los", "o_los", "f_This", "c_yTg", "c_yThi", "m_This", "m_xghi"))

        block = ctx.enter_context(nc.Block())

        @block.sync
        def _(sp):
            for a, src in ((0, ln_mix), (16, ln_ffn), (32, ssm_norm), (48, ssm_conv_b)):
                rows = src.rearrange("l (k p) -> (l k) p", p=P)
                sp.dma_start(vecs[a:a + rows.shape[0], :], rows).then_inc(vec_loaded, 16)
            sp.dma_start(cwr, ssm_conv_w[0].rearrange("j (k p) -> (j k) p", p=P)).then_inc(vec_loaded, 16)
            for t in range(TT):
                sp.dma_start(pos_i[:, t:t + 1], positions[0, t * P:(t + 1) * P].unsqueeze(1)
                             ).then_inc(pos_loaded, 16)
            for n, pieces in enumerate(stream):
                if n == 2:
                    sp.dma_start(brow[0:1, :], swa_b_qkv).then_inc(bias_loaded, 16)
                if n >= RING:
                    sp.wait_ge(lo_ready, n - RING + 1)
                for src, k, a, w in pieces:
                    width = sum(p[3] for p in pieces)
                    dst = ring[:, n % RING, 0:k * width].rearrange("p (k n) -> p k n", n=width)
                    sp.dma_start(dst[:, :, a:a + w], src).then_inc(slot_loaded[n % RING], 16)
            sp.wait_ge(r_passes, 1)
            passes = sp.value_load(passes_i[0:1, 0:1], min_val=E, max_val=2 * E)
            with sp.Fori(0, passes, E) as first:
                with sp.Fori(0, E) as e:
                    for c in range(LAYER_CHUNKS):
                        sp.wait_ge(lo_ready, (first + e) * LAYER_CHUNKS + (MOE0 + c - RING + 1))
                        if c < 4 * NJ:
                            src = block_of(moe_w_gu[0, e], (c % 2) * 4, 4, (c // 2 % 2) * FF + (c // 4) * 512, 512)
                        else:
                            src = block_of(moe_w_down[0, e], 2 * (c - 4 * NJ), 2, 0, D)
                        dst = ring[:, c % RING, :].rearrange("p (k n) -> p k n", n=512 if c < 4 * NJ else D)
                        sp.dma_start(dst, src).then_inc(slot_loaded[c % RING], 16)
            for c in range(AHEAD):
                sp.wait_ge(lo_ready, passes * LAYER_CHUNKS + (MOE0 + c - RING + 1))
                sp.dma_start(ring[:, c % RING, :].rearrange("p (k n) -> p k n", n=512),
                             block_of(moe_w_gu[0, 0], 4 * c, 4, 0, 512)).then_inc(slot_loaded[c % RING], 16)
            sp.wait_ge(out_ready, TT)
            sp.dma_start(out[0].rearrange("(t p) d -> p t d", p=P), xs[:]).then_inc(out_stored, 16)
            sp.wait_ge(out_stored, 16)

        @block.gpsimd
        def _(pool_e):
            pool_e.memset(ident[:], 0.0)
            pool_e.memset(tri[:], 1.0)
            pool_e.memset(tri_lt[:], 1.0)
            pool_e.memset(ones[:], 1.0)
            pool_e.memset(jlt[:], 1.0)
            for i in range(NF):
                pool_e.memset(invf[:, i:i + 1], float(np.float32(THETA ** (-2.0 * i / ROT))))
            pool_e.iota(places[:], [[1, P]], base=0, channel_multiplier=0,
                        allow_small_or_imprecise_dtypes=True)
            pool_e.drain()
            pool_e.affine_select(out=ident[:], in_=ident[:], compare_op=ALU.not_equal, fill=1.0, base=0,
                                 pattern=[[-1, P]], channel_multiplier=1)
            pool_e.affine_select(out=tri[:], in_=tri[:], compare_op=ALU.is_ge, fill=0.0, base=0,
                                 pattern=[[1, P]], channel_multiplier=-1)
            pool_e.affine_select(out=tri_lt[:], in_=tri_lt[:], compare_op=ALU.is_ge, fill=0.0, base=-1,
                                 pattern=[[1, P]], channel_multiplier=-1)
            pool_e.affine_select(out=jlt[:], in_=jlt[:], compare_op=ALU.is_ge, fill=0.0, base=-1,
                                 pattern=[[1, E], [-1, E]], channel_multiplier=0)
            pool_e.drain()
            pool_e.memset(flag[:], 0.0).then_inc(const_ready, 1)
            for dst, src in ((sinks_in, swa_sinks), (dtb, ssm_dt_bias), (alog, ssm_a_log), (dsk, ssm_d)):
                pool_e.dma_start(dst[:], src[0].partition_broadcast(P)).then_inc(bc_loaded, 16)
            pool_e.dma_start(rw[:], moe_w_router[0].rearrange("(k p) e -> p k e", p=P)).then_inc(bc_loaded, 16)
            pool_e.dma_start(dtw[:], block_of(ssm_w_in[0], 0, KD, C0 + G * N, SH)).then_inc(dtw_loaded, 16)

        @block.scalar
        def _(act):
            act.dma_start(h[:], x[0].rearrange("(t p) d -> p t d", p=P)).then_inc(x_loaded, 16)

            def norm(q, ready, at_least):
                act.wait_ge(ready, at_least)
                for t in range(TT):
                    act.activation(xs[:, t, :], h[:, t, :], ACT.Square,
                                   accum_out=st[:, q, t:t + 1]).then_inc(sq_done, 1)
                act.wait_ge(var_done, q + 1)
                act.activation(st[:, q, 4:6], st[:, q, 2:4], ACT.Sqrt).then_inc(sqrt_done, 1)

            split = [0]

            def ahead(n):
                while split[0] <= min(n, MOE0 - 1):
                    m = split[0]
                    act.wait_ge(slot_loaded[m % RING], loads_until(m))
                    if m >= SPLIT:
                        act.wait_ge(chunk_used, m - SPLIT + 1)
                    w = sum(p[3] * p[1] for p in stream[m])
                    act.activation(w_hi[:, m % SPLIT, 0:w], ring[:, m % RING, 0:w], ACT.Copy).then_inc(hi_ready, 1)
                    split[0] += 1

            def norm_hi(q):
                for i in range(4):
                    act.wait_ge(hT_done, 4 * q + i + 1)
                    part = (slice(None), slice((i % 2) * 4, (i % 2) * 4 + 4), slice((i // 2) * P, (i // 2 + 1) * P))
                    act.activation(hT_hi[part], hT[part], ACT.Copy).then_inc(hT_his, 1)

            norm(0, x_loaded, 16)
            ahead(1)
            act.wait_ge(angle_done, 1)
            act.activation(trig[:, 3], trig[:, 2], ACT.Sin).then_inc(trig_done, 1)
            norm_hi(0)
            for n, w in enumerate((512, 512, 256)):
                for t in range(TT):
                    ahead(QKV0 + 2 * n + 3)
                    act.wait_ge(*((qkv_mm, n + 1), (chunk_used, QKV0 + 2 * n + 2))[t])
                    act.activation(qkv[:, t, 512 * n:512 * n + w], bank[3 * t + n][:, 0:w],
                                   ACT.Copy).then_inc(qkv_sb, 1)
            for t in range(TT):
                for i in range(3):
                    act.wait_ge(qkT_mm, 3 * t + i + 1)
                    w = 4 if i < 2 else KV
                    dst = (qT[:, 4 * i:4 * i + 4, t * P:(t + 1) * P] if i < 2 else kT[:, :, t * P:(t + 1) * P])
                    act.activation(dst, bank[3 * t + i][:, 0:w * P].rearrange("p (a b) -> p a b", b=P),
                                   ACT.Copy).then_inc(qkT_sb, 1)
            for t in range(TT):
                act.wait_ge(sm_sub, t + 1)
                act.activation(prob[:, t], prob[:, t], ACT.Exp)
                act.activation(sm[:, t, 2], sm[:, t, 2], ACT.Exp).then_inc(sm_exp, 1)
            for t in range(TT):
                if t == 1:
                    act.wait_ge(o_mm, 1)
                for i in range(4):
                    act.wait_ge(pT_mm, 4 * t + i + 1)
                    act.activation(pT[:, 4 * i:4 * i + 4, :], bank[4 * t + i][:].rearrange("p (a b) -> p a b", b=P),
                                   ACT.Copy).then_inc(pT_sb, 1)
                act.wait_ge(o_mm, t + 1)
                for i in range(2):
                    act.activation(oT_hi[:, 4 * i:4 * i + 4, t * P:(t + 1) * P],
                                   bank[2 * t + i][:].rearrange("p (a b) -> p a b", b=P),
                                   ACT.Copy).then_inc(o_sb, 1)
            ahead(WO0 + 5)
            norm(1, h_done, 4)
            ahead(FGU0 + 2)
            norm_hi(1)
            for j in range(NJ + 1):
                for b in range(TT):
                    if j < NJ:
                        ahead(FGU0 + 4 * j + 3)
                        act.wait_ge(*((f_gate, j + 1), (chunk_used, FGU0 + 4 * j + 2))[b])
                        if j >= 1:
                            act.wait_ge(f_h, 2 * (j - 1) + b + 1)
                        act.activation(f_sg[:, b], bank[b][:], ACT.Silu).then_inc(f_silu, 1)
                    else:
                        ahead(FDN0 + 1)
                if j >= 1:
                    for b in range(TT):
                        act.wait_ge(f_T, 2 * (j - 1) + b + 1)
                        act.activation(f_hT_hi[:, 4 * (j - 1):4 * j, b * P:(b + 1) * P],
                                       bank[4 + b][:].rearrange("p (a b) -> p a b", b=P),
                                       ACT.Copy).then_inc(f_This, 1)
            ahead(Z0)
            norm(2, h_done, 8)
            ahead(Z0 + 2)
            norm_hi(2)
            act.wait_ge(bc_loaded, 5 * 16)
            act.activation(dts[:, 5, 0:SH], alog[:], ACT.Exp).then_inc(c_ea, 1)
            act.wait_ge(c_nabs, 1)
            act.activation(dts[:, 2], dts[:, 1], ACT.Exp).then_inc(c_e, 1)
            act.wait_ge(c_u1, 1)
            act.activation(dts[:, 4], dts[:, 3], ACT.Ln).then_inc(c_ln, 1)
            for n in range(4):
                for t in range(TT):
                    i = 2 * n + t
                    ahead(Z0 + 2 * n + 3)
                    act.wait_ge(*((c_z, n + 1), (chunk_used, Z0 + 2 * n + 2))[t])
                    act.activation(z[:, t, 512 * n:512 * (n + 1)], bank[i % 4][:], ACT.Silu).then_inc(c_zs, 1)
            act.wait_ge(c_pad, 1)
            for s in range(G + 1):
                if s < G:
                    for i in range(2):
                        ahead(GR0 + 2 * s + 3)
                        act.wait_ge(*((c_proj, s + 1), (chunk_used, GR0 + 2 * s + 2))[i])
                        if s >= 1:
                            act.wait_ge(c_conv, s)
                        act.activation(U[:, 2 * i:2 * i + 2, 3:], bank[i][:].rearrange("p (a b) -> p a b", b=T),
                                       ACT.Copy).then_inc(c_u, 1)
                    act.wait_ge(c_conv, s + 1)
                    if s >= 1:
                        act.wait_ge(c_cb, s)
                    for i, ct in enumerate((2 * s, 2 * s + 1, KI + s, KI + G + s)):
                        act.activation(XC[:, i], acc[:, i], ACT.Silu,
                                       bias=vT[:, 48 + ct:49 + ct]).then_inc(c_xc, 1)
                if s >= 1:
                    act.wait_ge(c_arg, s)
                    act.activation(arg[:], arg[:], ACT.Exp).then_inc(c_exp, 1)
            act.wait_ge(c_gated, 1)
            for t in range(TT):
                act.activation(z[:, t], y[:, t], ACT.Square, accum_out=st[:, 4, t:t + 1]).then_inc(c_sq, 1)
            act.wait_ge(c_var, 1)
            act.activation(st[:, 4, 4:6], st[:, 4, 2:4], ACT.Sqrt).then_inc(c_sqrt, 1)
            for i in range(8):
                act.wait_ge(c_yTg, i + 1)
                act.activation(yT_hi[:, 4 * (i % 4):4 * (i % 4) + 4, (i // 4) * P:(i // 4 + 1) * P],
                               yT[:, i % 2].rearrange("p (a b) -> p a b", b=P), ACT.Copy).then_inc(c_yThi, 1)
            ahead(MOE0 - 1)
            norm(3, h_done, 12)
            for t in range(TT):
                act.wait_ge(xs_done, 6 + t + 1)
                act.activation(xs_hi[:, t], xs[:, t], ACT.Copy).then_inc(xs_his, 1)
            act.dma_start(gfin, ln_final.partition_broadcast(P)).then_inc(gain_loaded, 16)
            act.wait_ge(r_max, 1)
            act.activation(rt[:, 2], rt[:, 1], ACT.Exp).then_inc(r_exp, 1)
            act.wait_ge(r_passes, 1)
            passes = act.value_load(passes_i[0:1, 0:1], min_val=E, max_val=2 * E)

            def gathered(at):
                for k in range(KD):
                    if k % 4 == 0:
                        act.wait_ge(m_gath, at * 2 + (k // 4 + 1))
                    ins = act.activation(xgT_hi[:, k], bank[6 + k // 4][:, (k % 4) * P:(k % 4 + 1) * P], ACT.Copy,
                                         scale=vT[:, 24 + k:25 + k])
                ins.then_inc(m_xghi, 1)

            gathered(0)
            act.sem_inc(m_silu, 1)

            def ahead_e(at, a, b):
                for c in range(a, min(b, LAYER_CHUNKS)):
                    act.wait_ge(slot_loaded[c % RING], at * (LAYER_CHUNKS // RING * 16)
                                + (slot_base[c % RING] + 16 * (c // RING + 1)))
                    act.wait_ge(chunk_used, at * LAYER_CHUNKS + (MOE0 + c - SPLIT + 1))
                    act.activation(w_hi[:, c % SPLIT], ring[:, c % RING], ACT.Copy).then_inc(hi_ready, 1)

            ahead_e(0, 0, AHEAD)
            with act.Fori(0, passes) as it:
                for j in range(NJ):
                    ahead_e(it, max(4 * j, AHEAD), 4 * j + 4)
                    act.wait_ge(chunk_used, it * LAYER_CHUNKS + (MOE0 + 4 * j + 2))
                    act.wait_ge(m_h, it * NJ + (1 + j))
                    act.activation(m_sg[:, 0], bank[0][:], ACT.Silu).then_inc(m_silu, 1)
                    if j >= 1:
                        act.wait_ge(m_T, it * NJ + (1 + j))
                        act.activation(m_hT_hi[:, 4 * (j - 1):4 * j, :],
                                       bank[4 + (j - 1) % 2][:].rearrange("p (a b) -> p a b", b=P),
                                       ACT.Copy).then_inc(m_This, 1)
                ahead_e(it, 4 * NJ, 4 * NJ + 3)
                gathered(it + 1)
                ahead_e(it, 4 * NJ + 3, 6 * NJ - 1)
                act.wait_ge(m_T, it * NJ + (1 + NJ))
                act.activation(m_hT_hi[:, KF - 4:KF, :], bank[4 + (NJ - 1) % 2][:].rearrange("p (a b) -> p a b", b=P),
                               ACT.Copy).then_inc(m_This, 1)
                ahead_e(it, 6 * NJ - 1, 6 * NJ)
                ahead_e(it + 1, 0, AHEAD)
                for i in range(2):
                    act.wait_ge(*((m_y, it + 1), (chunk_used, it * LAYER_CHUNKS + (MOE0 + LAYER_CHUNKS)))[i])
                    act.activation(yg[:, 512 * i:512 * (i + 1)], bank[2 + i][:], ACT.Copy).then_inc(m_ysb, 1)
            act.wait_ge(var_done, 5)
            act.activation(st[:, 4, 4:6], st[:, 4, 2:4], ACT.Sqrt).then_inc(sqrt_done, 1)

        @block.tensor
        def _(pe):
            def product(o, stat, mov, start, stop):
                pe.matmul(o, stat[0], mov[0], start=start, stop=False)
                pe.matmul(o, stat[0], mov[1], start=False, stop=False)
                return pe.matmul(o, stat[1], mov[0], start=False, stop=stop)

            def part(pair, *at):
                return tuple(v[(slice(None), *at)] for v in pair)

            def have(n):
                pe.wait_ge(lo_ready, n + 1)

            hTs = (hT_hi, hT_lo)

            pe.wait_ge(const_ready, 1)
            pe.wait_ge(vec_loaded, 5 * 16)
            pe.transpose(bank[0][:, 0:80], vecs[0:80, :], ident[0:80, 0:80])
            pe.transpose(bank[0][:, P:2 * P], cwr[:], ident[:]).then_inc(vec_T, 1)

            def norm_T(q):
                for t in range(TT):
                    pe.wait_ge(xs_done, 2 * q + t + 1)
                    for k in range(KD):
                        ins = pe.transpose(bank[4 + 2 * t + k // 4][:, (k % 4) * P:(k % 4 + 1) * P],
                                           xs[:, t, k * P:(k + 1) * P], ident[:])
                        if k % 4 == 3:
                            ins.then_inc(xT_mm, 1)

            norm_T(0)
            pe.wait_ge(bias_loaded, 16)
            pe.wait_ge(vec_sb, 1)
            pe.wait_ge(hT_los, 4)
            for n, w in enumerate((512, 512, 256)):
                for t in range(TT):
                    pe.matmul(bank[3 * t + n][:, 0:w], ones[0:1, :], brow[0:1, 512 * n:512 * n + w],
                              start=True, stop=False)
                for half in range(2):
                    have(QKV0 + 2 * n + half)
                    wv = part(chunk(QKV0 + 2 * n + half, w), slice(0, 4))
                    for t in range(TT):
                        o = bank[3 * t + n][:, 0:w]
                        for k in range(4):
                            ins = product(o, part(hTs, 4 * half + k, slice(t * P, (t + 1) * P)), part(wv, k),
                                          False, half == 1 and k == 3)
                        if t == 1 or half == 1:
                            ins.then_inc((qkv_mm, chunk_used)[t], 1)
            for t in range(TT):
                pe.wait_ge(rope_done, t + 1)
                for i in range(3):
                    for a in range(4 if i < 2 else KV):
                        src = (qkv[:, t, (4 * i + a) * P:(4 * i + a + 1) * P] if i < 2 else
                               kd[:, t, a].rearrange("p a b -> p (a b)"))
                        ins = pe.transpose(bank[3 * t + i][:, a * P:(a + 1) * P], src, ident[:])
                    ins.then_inc(qkT_mm, 1)
            pe.wait_ge(qkT_sb, 6)
            for t in range(TT):
                for hd in range(HEADS):
                    s = place_of(hd)
                    r = slice((hd % 2) * HD, (hd % 2 + 1) * HD)
                    kv = hd // (HEADS // KV)
                    for c in (2 * t, 2 * t + 1):
                        half = c % 2
                        keys = {0: (0, 0), 1: (0, 1), 2: (2, 1), 3: (2, 3)}[c]
                        for i, kc in enumerate(keys):
                            ins = pe.matmul(
                                bank[4 * t + s // 4][half * CH:(half + 1) * CH,
                                                      (s % 4) * P + i * CH:(s % 4) * P + (i + 1) * CH],
                                qT[r, hd // 2, c * CH:(c + 1) * CH], kT[r, kv, kc * CH:(kc + 1) * CH],
                                start=True, stop=True)
                ins.then_inc(s_mm, 1)
            for t in range(TT):
                pe.wait_ge(p_ready, t + 1)
                for s in range(HEADS):
                    ins = pe.transpose(bank[4 * t + s // 4][:, (s % 4) * P:(s % 4 + 1) * P], prob[:, t, s],
                                       ident[:])
                    if s % 4 == 3:
                        ins.then_inc(pT_mm, 1)
                pe.wait_ge(pT_sb, 4 * (t + 1))
                for hd in range(HEADS):
                    kv = hd // (HEADS // KV)
                    for c in (2 * t, 2 * t + 1):
                        v = (vmid[:, kv * HD:(kv + 1) * HD] if c == 2 else
                             qkv[:, t, (HEADS + KV + kv) * HD:(HEADS + KV + kv + 1) * HD])
                        pair = hd // 2
                        ins = pe.matmul(bank[2 * t + pair // 4][(hd % 2) * HD:(hd % 2 + 1) * HD,
                                                               (pair % 4) * P + (c % 2) * CH:
                                                               (pair % 4) * P + (c % 2 + 1) * CH],
                                        v, pT[:, place_of(hd), (c % 2) * CH:(c % 2 + 1) * CH], start=True, stop=True)
                ins.then_inc(o_mm, 1)
            def times_1024(n, stat, outs, done):
                for half in range(2):
                    have(n + half)
                    wv = chunk(n + half, 512)
                    for t in range(TT):
                        for k in range(4):
                            ins = product(outs[t], part(stat, 4 * half + k, slice(t * P, (t + 1) * P)),
                                          part(wv, k), half == 0 and k == 0, half == 1 and k == 3)
                        if t == 1 or half == 1:
                            ins.then_inc((done, chunk_used)[t], 1)

            pe.wait_ge(o_los, 4)
            for n in range(2):
                times_1024(WO0 + 2 * n, (oT_hi, oT_lo), [bank[4 + 2 * n + t][:] for t in range(TT)], wo_mm)

            norm_T(1)
            pe.wait_ge(hT_los, 8)

            def f_transposes(j):
                for b in range(TT):
                    pe.wait_ge(f_h, 2 * j + b + 1)
                    if j >= 1:
                        pe.wait_ge(f_Tsb, 2 * (j - 1) + b + 1)
                    for a in range(4):
                        ins = pe.transpose(bank[4 + b][:, a * P:(a + 1) * P], f_hh[:, b, a * P:(a + 1) * P],
                                           ident[:])
                    ins.then_inc(f_T, 1)

            for j in range(NJ):
                for gu, done in ((0, f_gate), (1, f_up)):
                    if j >= 1:
                        pe.wait_ge((f_silu, f_h)[gu], 2 * j)
                    times_1024(FGU0 + 4 * j + 2 * gu, hTs, [bank[2 * gu + b][:] for b in range(TT)], done)
                    if gu == 0 and j >= 1:
                        f_transposes(j - 1)
            f_transposes(NJ - 1)

            def times_rows(n, stat, k_tiles):
                for c in range(k_tiles // 2):
                    have(n + c)
                    wv = chunk(n + c, D)
                    for k in range(2):
                        for t in range(TT):
                            for i in range(2):
                                ins = product(bank[2 * t + i][:], part(stat, 2 * c + k, slice(t * P, (t + 1) * P)),
                                              part(wv, k, slice(512 * i, 512 * (i + 1))), c == 0 and k == 0,
                                              c == k_tiles // 2 - 1 and k == 1)
                    ins.then_inc(chunk_used, 1)

            pe.wait_ge(f_Tsb, 2 * NJ)
            times_rows(FDN0, (f_hT_hi, f_hT_lo), KF)

            norm_T(2)
            pe.wait_ge(hT_done, 12)
            pe.wait_ge(dtw_loaded, 16)
            for t in range(TT):
                for k in range(KD):
                    ins = pe.matmul(bank[6][:, t * SH:(t + 1) * SH], hT[:, k, t * P:(t + 1) * P], dtw[:, k, :],
                                    start=(k == 0), stop=(k == KD - 1))
            ins.then_inc(c_dt, 1)
            pe.wait_ge(hT_los, 12)
            for n in range(4):
                if n >= 2:
                    pe.wait_ge(c_zs, 2 * n - 2)
                times_1024(Z0 + 2 * n, hTs, [bank[(2 * n + t) % 4][:] for t in range(TT)], c_z)
            pe.wait_ge(c_dtA, 1)
            dtA = dts[:, 8].rearrange("p (t h) -> p t h", t=TT)
            pe.matmul(bank[7][:, 0:SH], tri[:], dtA[:, 0, :], start=True, stop=True)
            pe.matmul(bank[7][:, SH:2 * SH], tri[:], dtA[:, 1, :], start=True, stop=True)
            pe.matmul(bank[7][:, 2 * SH:3 * SH], ones[:], dtA[:, 0, :], start=True, stop=True).then_inc(c_acol, 1)
            pe.wait_ge(c_zs, 8)
            for s in range(G + 2):
                if s < G:
                    if s >= 1:
                        pe.wait_ge(c_u, 2 * s)
                    for half in range(2):
                        have(GR0 + 2 * s + half)
                        wv = chunk(GR0 + 2 * s + half, 512)
                        for i in range(4):
                            for k in range(4):
                                ins = product(bank[i // 2][:, (i % 2) * T:(i % 2 + 1) * T],
                                              part(wv, k, slice(i * P, (i + 1) * P)), part(hTs, 4 * half + k),
                                              half == 0 and k == 0 and i % 2 == 0,
                                              half == 1 and k == 3 and i % 2 == 1)
                            if i == 3 or (i == 1 and half == 1):
                                ins.then_inc((c_proj, chunk_used)[i // 2], 1)
                g = s - 2
                if g >= 0:
                    pe.wait_ge(c_m, g + 1)
                    if g >= 1:
                        pe.wait_ge(c_yadd, g)
                    for r in range(REP):
                        xr = slice(r * 64, (r + 1) * 64)
                        pe.matmul(bank[6][:, r * 64:(r + 1) * 64], M[:, 0, r], Xdt[:, 0, xr],
                                  start=True, stop=True)
                        pe.matmul(bank[6][:, (REP + r) * 64:(REP + r + 1) * 64], M[:, 1, r], Xdt[:, 0, xr],
                                  start=True, stop=False)
                        ins = pe.matmul(bank[6][:, (REP + r) * 64:(REP + r + 1) * 64], M[:, 2, r],
                                        Xdt[:, 1, xr], start=False, stop=True)
                    ins.then_inc(c_y, 1)
                g = s - 1
                if 0 <= g < G:
                    if g >= 1:
                        pe.wait_ge(c_arg, g)
                    for t in range(TT):
                        for r in range(REP):
                            ins = pe.matmul(bank[4 + t][:, r * P:(r + 1) * P],
                                            dtA[:, t, g * REP + r:g * REP + r + 1].to_broadcast([P, P]), tri[:],
                                            start=True, stop=True)
                    ins.then_inc(c_abc, 1)
                    pe.wait_ge(c_xc, 4 * (g + 1))
                    if g >= 1:
                        pe.wait_ge(c_xd, 2 * g)
                    for t in range(TT):
                        for i in range(2):
                            ins = pe.transpose(bank[2][:, t * T + i * P:t * T + (i + 1) * P],
                                               XC[:, i, t * P:(t + 1) * P], ident[:])
                    ins.then_inc(c_xT, 1)
                    pe.matmul(bank[3][:, 0:T], XC[:, 2, 0:P], XC[:, 3, :], start=True, stop=True)
                    pe.matmul(bank[3][:, T:T + P], XC[:, 2, P:T], XC[:, 3, P:T], start=True,
                              stop=True).then_inc(c_cb, 1)
            for t in range(TT):
                pe.wait_ge(c_yn, t + 1)
                for k in range(KI):
                    b = k // 4 % 4
                    i = 4 * t + k // 4
                    if k % 4 == 0 and i >= 4:
                        pe.wait_ge(c_yTsb, i - 3)
                    ins = pe.transpose(bank[4 + b][:, (k % 4) * P:(k % 4 + 1) * P], y[:, t, k * P:(k + 1) * P],
                                       ident[:])
                    if k % 4 == 3:
                        ins.then_inc(c_yT, 1)
            pe.wait_ge(c_yTsb, 8)
            times_rows(SO0, (yT_hi, yT_lo), KI)

            norm_T(3)
            pe.wait_ge(hT_done, 16)
            pe.wait_ge(bc_loaded, 5 * 16)
            for t in range(TT):
                for k in range(KD):
                    ins = pe.matmul(bank[0][:, t * E:(t + 1) * E], hT[:, k, t * P:(t + 1) * P], rw[:, k, :],
                                    start=(k == 0), stop=(k == KD - 1))
            ins.then_inc(r_logit, 1)
            pe.wait_ge(r_sel, 1)
            chosen = rt[:, 5].rearrange("p (t e) -> p t e", t=TT)
            pe.matmul(bank[1][:, 0:E], tri_lt[:], chosen[:, 0, :], start=True, stop=True)
            pe.matmul(bank[1][:, E:2 * E], ones[:], chosen[:, 0, :], start=True, stop=False)
            pe.matmul(bank[1][:, E:2 * E], tri_lt[:], chosen[:, 1, :], start=False, stop=True)
            pe.matmul(bank[1][:, 2 * E:3 * E], ones[:], chosen[:, 0, :], start=True, stop=False)
            pe.matmul(bank[1][:, 2 * E:3 * E], ones[:], chosen[:, 1, :], start=False, stop=True).then_inc(r_cnt, 1)
            pe.wait_ge(r_passes, 1)
            passes = pe.value_load(passes_i[0:1, 0:1], min_val=E, max_val=2 * E)

            def gather(at):
                pe.wait_ge(m_S, at + 2)
                if not isinstance(at, int):
                    pe.wait_ge(m_add, at * 2 + 1)
                for k in range(KD):
                    for t in range(TT):
                        o = bank[6 + k // 4][:, (k % 4) * P:(k % 4 + 1) * P]
                        pe.matmul(o, xs_hi[:, t, k * P:(k + 1) * P], sel[:, t], start=(t == 0), stop=False)
                        ins = pe.matmul(o, xs_lo[:, t, k * P:(k + 1) * P], sel[:, t], start=False, stop=(t == 1))
                    if k % 4 == 3:
                        ins.then_inc(m_gath, 1)

            pe.sem_inc(m_T, 1)
            pe.sem_inc(m_gt, 1)
            pe.wait_ge(xs_los, TT)
            gather(-1)

            def combine(at):
                pe.wait_ge(m_gtsb, at + 1)
                pe.wait_ge(m_ysb, at * 2 + 2)
                for t in range(TT):
                    for i in range(2):
                        ins = pe.matmul(bank[(6, 2)[t] + i][:], gselT[:, t], yg[:, 512 * i:512 * (i + 1)],
                                        start=True, stop=True)
                    ins.then_inc(m_comb, 1)

            with pe.Fori(0, passes) as it:
                def have_e(c):
                    pe.wait_ge(lo_ready, it * LAYER_CHUNKS + (MOE0 + c + 1))

                def m_transposes(j):
                    pe.wait_ge(m_h, it * NJ + (1 + j + 1))
                    pe.wait_ge(m_Tsb, it * NJ + (1 + max(j - 1, 0)))
                    for a in range(4):
                        ins = pe.transpose(bank[4 + j % 2][:, a * P:(a + 1) * P], m_hh[:, 0, a * P:(a + 1) * P],
                                           ident[:])
                    ins.then_inc(m_T, 1)

                pe.wait_ge(m_xg, it + 1)
                for j in range(NJ):
                    for gu in range(2):
                        pe.wait_ge((m_silu, m_h)[gu], it * NJ + (1 + j))
                        if j == 0 and gu == 0:
                            pe.wait_ge(m_gtsb, it + 1)
                        for half in range(2):
                            c = 4 * j + 2 * gu + half
                            have_e(c)
                            wv = chunk(c, 512)
                            for k in range(4):
                                ins = product(bank[gu][:], part((xgT_hi, xgT_lo), 4 * half + k), part(wv, k),
                                              half == 0 and k == 0, half == 1 and k == 3)
                            ins.then_inc(chunk_used, 1)
                        if gu == 0:
                            m_transposes(j - 1) if j >= 1 else combine(it)
                gather(it)
                pe.wait_ge(m_add, it * 2 + 2)
                for c in range(2 * NJ):
                    if c == 2 * NJ - 2:
                        m_transposes(NJ - 1)
                        pe.wait_ge(m_gs, it + 1)
                        pe.wait_ge(m_silu, it * NJ + (1 + NJ))
                        for t in range(TT):
                            ins = pe.transpose(bank[0][:, t * P:(t + 1) * P], gsel[:, t], ident[:])
                        ins.then_inc(m_gt, 1)
                    have_e(4 * NJ + c)
                    wv = chunk(4 * NJ + c, D)
                    pe.wait_ge(m_Tsb, it * NJ + (1 + c // 2 + 1))
                    for k in range(2):
                        for i in range(2):
                            ins = product(bank[2 + i][:], part((m_hT_hi, m_hT_lo), 2 * c + k),
                                          part(wv, k, slice(512 * i, 512 * (i + 1))), c == 0 and k == 0,
                                          c == 2 * NJ - 1 and k == 1)
                            if c == 2 * NJ - 1 and k == 1 and i == 0:
                                ins.then_inc(m_y, 1)
                    ins.then_inc(chunk_used, 1)
            combine(passes)

        @block.vector
        def _(dve):
            def root(q, n, src, var, rooted, v_inc, rooted_at):
                s, v, r, i, u = (src[:, 2 * a:2 * a + 2] for a in (0, 1, 2, 3, 0))
                dve.tensor_scalar(v, s, 1.0 / n, EPS, ALU.mult, ALU.add).then_inc(var, v_inc)
                dve.wait_ge(rooted, rooted_at)
                dve.reciprocal(i, r)
                dve.drain()
                dve.tensor_tensor(u, i, i, ALU.mult)
                dve.drain()
                dve.tensor_tensor(u, u, v, ALU.mult)
                dve.drain()
                dve.tensor_scalar(u, u, -0.5, 1.5, ALU.mult, ALU.add)
                dve.drain()
                dve.tensor_tensor(i, i, u, ALU.mult)
                dve.drain()
                return i

            def norm(q, gain_at):
                dve.wait_ge(sq_done, 2 * q + 2)
                i = root(q, D, st[:, q], var_done, sqrt_done, 1, q + 1)
                for t in range(TT):
                    dve.tensor_scalar(xs[:, t, :], h[:, t, :], i[:, t:t + 1], None, ALU.mult).then_inc(xs_done, 1)
                for t in range(TT):
                    for k in (0, 4):
                        dve.wait_ge(xT_mm, 4 * q + 2 * t + k // 4 + 1)
                        dve.tensor_tensor(hT[:, k:k + 4, t * P:(t + 1) * P],
                                          bank[4 + 2 * t + k // 4][:].rearrange("p (a b) -> p a b", b=P),
                                          vT[:, gain_at + k:gain_at + k + 4].unsqueeze(2).to_broadcast([P, 4, P]),
                                          ALU.mult).then_inc(hT_done, 1)
                        if q < 3 and (t, k) != (0, 0):
                            norm_lo(q, 2 * t + k // 4 - 1)
                if q < 3:
                    norm_lo(q, 3)

            def norm_lo(q, i):
                dve.wait_ge(hT_his, 4 * q + i + 1)
                part = (slice(None), slice((i % 2) * 4, (i % 2) * 4 + 4), slice((i // 2) * P, (i // 2 + 1) * P))
                dve.tensor_tensor(hT_lo[part], hT[part], hT_hi[part].bitcast(F32), ALU.subtract).then_inc(hT_los, 1)

            split = [0]

            def ahead(n):
                while split[0] <= min(n, MOE0 - 1):
                    m = split[0]
                    dve.wait_ge(hi_ready, m + 1)
                    w = sum(p[3] * p[1] for p in stream[m])
                    dve.tensor_tensor(w_lo[:, m % SPLIT, 0:w], ring[:, m % RING, 0:w],
                                      w_hi[:, m % SPLIT, 0:w].bitcast(F32), ALU.subtract).then_inc(lo_ready, 1)
                    split[0] += 1

            dve.wait_ge(vec_T, 1)
            dve.tensor_copy(vT[:, 0:80], bank[0][:, 0:80])
            dve.tensor_copy(cwT[:].rearrange("p a b -> p (a b)"), bank[0][:, P:2 * P]).then_inc(vec_sb, 1)
            dve.wait_ge(pos_loaded, 32)
            dve.wait_ge(const_ready, 1)
            posf = rt[:, 0, 0:TT]
            dve.tensor_copy(posf, pos_i[:])
            dve.drain()
            for t in range(TT):
                for i in range(2):
                    dve.tensor_scalar(trig[:, 0, t, i * NF:(i + 1) * NF], invf[:], posf[:, t:t + 1], None, ALU.mult)
            dve.drain()
            for i, quarter in ((0, 0.0), (1, 0.25)):
                f = slice(i * NF, (i + 1) * NF)
                dve.tensor_scalar(trig[:, 1, :, f], trig[:, 0, :, f], 1.0 / (2 * math.pi), quarter, ALU.mult, ALU.add)
            dve.drain()
            dve.tensor_scalar(trig[:, 1], trig[:, 1], 12582912.0, None, ALU.add)
            dve.drain()
            dve.tensor_scalar(trig[:, 1], trig[:, 1], 12582912.0, None, ALU.subtract)
            dve.drain()
            left, src = 2 * math.pi, trig[:, 0]
            for bits in (5, 13, 21, 60):
                part = float(np.float32(left)) if bits == 60 else math.floor(left * 2.0 ** bits) / 2.0 ** bits
                left -= part
                dve.scalar_tensor_tensor(trig[:, 2], trig[:, 1], -part, src, ALU.mult, ALU.add)
                dve.drain()
                src = trig[:, 2]
            dve.tensor_scalar(trig[:, 2, :, NF:], trig[:, 2, :, NF:], math.pi / 2, None, ALU.add)
            dve.drain()
            dve.tensor_scalar(trig[:, 2], trig[:, 2], -3.1415925, 3.1415925, ALU.max, ALU.min).then_inc(angle_done, 1)

            norm(0, 0)
            ahead(QKV0 + 7)
            dve.wait_ge(trig_done, 1)
            tmp = rtmp.rearrange("p (a h f) -> p a h f", a=4, f=NF)
            for t in range(TT):
                dve.wait_ge(qkv_sb, 5 + t)
                heads = qkv[:, t, 0:(HEADS + KV) * HD].rearrange("p (h d) -> p h d", d=HD)
                t1, t2 = heads[:, :, 0:NF], heads[:, :, NF:2 * NF]
                sn = trig[:, 3, t, 0:NF].unsqueeze(1).to_broadcast([P, HEADS + KV, NF])
                cs = trig[:, 3, t, NF:].unsqueeze(1).to_broadcast([P, HEADS + KV, NF])
                for i, (a, b) in enumerate(((t1, cs), (t2, sn), (t2, cs), (t1, sn))):
                    dve.tensor_tensor(tmp[:, i], a, b, ALU.mult)
                dve.drain()
                dve.tensor_tensor(t1, tmp[:, 0], tmp[:, 1], ALU.subtract)
                dve.tensor_tensor(t2, tmp[:, 2], tmp[:, 3], ALU.add)
                dve.drain()
                for kv in range(KV):
                    ins = dve.tensor_copy(kd[:, t, kv], qkv[:, t, (HEADS + kv) * HD:(HEADS + kv + 1) * HD]
                                          .unsqueeze(1).to_broadcast([P, 2, HD]))
                src = qkv[(1 - t) * CH:(2 - t) * CH, t, (HEADS + KV) * HD:QKV]
                ins = dve.tensor_copy(vmid[(1 - t) * CH:(2 - t) * CH, :], src)
                ins.then_inc(rope_done, 1)
                dve.drain()
            scale = HD ** -0.5
            dve.wait_ge(bc_loaded, 5 * 16)
            dve.tensor_copy(sinks[:].rearrange("p (b a) -> p b a", b=2),
                            sinks_in[:].rearrange("p (a b) -> p b a", b=2))
            dve.drain()
            for t in range(TT):
                dve.wait_ge(s_mm, t + 1)
                for i in range(4):
                    dve.tensor_reduce(sm[:, t, 0, 4 * i:4 * i + 4],
                                      bank[4 * t + i][:].rearrange("p (a b) -> p a b", b=P), AXX, ALU.max)
                dve.drain()
                dve.scalar_tensor_tensor(sm[:, t, 1], sm[:, t, 0], scale, sinks[:], ALU.mult, ALU.max)
                dve.drain()
                dve.tensor_tensor(sm[:, t, 2], sinks[:], sm[:, t, 1], ALU.subtract)
                for i in range(4):
                    ins = dve.scalar_tensor_tensor(
                        prob[:, t, 4 * i:4 * i + 4], bank[4 * t + i][:].rearrange("p (a b) -> p a b", b=P), scale,
                        sm[:, t, 1, 4 * i:4 * i + 4].unsqueeze(2).to_broadcast([P, 4, P]), ALU.mult, ALU.subtract)
                ins.then_inc(sm_sub, 1)
            for t in range(TT):
                dve.wait_ge(sm_exp, t + 1)
                if t == 0:
                    dve.memset(prob[0:CH, 0, :, CH:], 0.0)
                    dve.drain()
                dve.tensor_reduce(sm[:, t, 3], prob[:, t], AXX, ALU.add)
                dve.drain()
                dve.tensor_tensor(sm[:, t, 3], sm[:, t, 3], sm[:, t, 2], ALU.add)
                dve.drain()
                dve.reciprocal(sm[:, t, 3], sm[:, t, 3])
                dve.drain()
                dve.tensor_tensor(prob[:, t], prob[:, t], sm[:, t, 3].unsqueeze(2).to_broadcast([P, HEADS, P]),
                                  ALU.mult).then_inc(p_ready, 1)
            for t in range(TT):
                for i in range(2):
                    dve.wait_ge(o_sb, 2 * t + i + 1)
                    part = (slice(None), slice(4 * i, 4 * i + 4), slice(t * P, (t + 1) * P))
                    dve.tensor_tensor(oT_lo[part], bank[2 * t + i][:].rearrange("p (a b) -> p a b", b=P),
                                      oT_hi[part].bitcast(F32), ALU.subtract).then_inc(o_los, 1)
            for n in range(2):
                ahead(WO0 + 2 * n + 3)
                for t in range(TT):
                    dve.wait_ge(*((wo_mm, n + 1), (chunk_used, WO0 + 2 * n + 2))[t])
                    hh = h[:, t, 512 * n:512 * (n + 1)]
                    dve.tensor_tensor(hh, hh, bank[4 + 2 * n + t][:], ALU.add).then_inc(h_done, 1)
            norm(1, 16)

            def f_lo(j):
                for b in range(TT):
                    dve.wait_ge(f_This, 2 * j + b + 1)
                    part = (slice(None), slice(4 * j, 4 * j + 4), slice(b * P, (b + 1) * P))
                    dve.tensor_tensor(f_hT_lo[part], bank[4 + b][:].rearrange("p (a b) -> p a b", b=P),
                                      f_hT_hi[part].bitcast(F32), ALU.subtract).then_inc(f_Tsb, 1)

            for j in range(NJ):
                ahead(FGU0 + 4 * j + 3)
                if j >= 1:
                    f_lo(j - 1)
                ahead(FGU0 + 4 * j + 5)
                for b in range(TT):
                    dve.wait_ge(*((f_up, j + 1), (chunk_used, FGU0 + 4 * j + 4))[b])
                    dve.wait_ge(f_silu, 2 * j + b + 1)
                    if j >= 1:
                        dve.wait_ge(f_T, 2 * (j - 1) + b + 1)
                    dve.tensor_tensor(f_hh[:, b], f_sg[:, b], bank[2 + b][:], ALU.mult).then_inc(f_h, 1)
            f_lo(NJ - 1)
            ahead(Z0)
            dve.wait_ge(chunk_used, FDN0 + KF // 2)
            for t in range(TT):
                for i in range(2):
                    hh = h[:, t, 512 * i:512 * (i + 1)]
                    dve.tensor_tensor(hh, hh, bank[2 * t + i][:], ALU.add).then_inc(h_done, 1)
            norm(2, 8)
            ahead(Z0 + 2)
            dve.memset(U[:, :, 0:3], 0.0).then_inc(c_pad, 1)
            dve.wait_ge(c_dt, 1)
            v2 = [dts[:, i] for i in range(12)]
            by_t = [dts[:, i].rearrange("p (t h) -> p t h", t=TT) for i in range(12)]
            dve.tensor_tensor(by_t[0], bank[6][:, 0:2 * SH].rearrange("p (t h) -> p t h", t=TT),
                              dtb[:].unsqueeze(1).to_broadcast([P, TT, SH]), ALU.add)
            dve.drain()
            dve.tensor_scalar(v2[1], v2[0], -1.0, None, ALU.mult)
            dve.drain()
            dve.tensor_tensor(v2[1], v2[1], v2[0], ALU.min).then_inc(c_nabs, 1)
            dve.wait_ge(c_e, 1)
            dve.tensor_scalar(v2[3], v2[2], 1.0, None, ALU.add).then_inc(c_u1, 1)
            dve.drain()
            dve.tensor_scalar(v2[6], v2[3], -1.0, None, ALU.add)
            dve.drain()
            dve.tensor_scalar(v2[7], v2[6], 0.0, None, ALU.is_equal)
            dve.drain()
            dve.tensor_tensor(v2[6], v2[6], v2[7], ALU.add)
            dve.drain()
            dve.reciprocal(v2[6], v2[6])
            dve.drain()
            dve.wait_ge(c_ln, 1)
            dve.tensor_tensor(v2[6], v2[6], v2[4], ALU.mult)
            dve.drain()
            dve.tensor_tensor(v2[6], v2[6], v2[7], ALU.add)
            dve.drain()
            dve.tensor_tensor(v2[6], v2[6], v2[2], ALU.mult)
            dve.drain()
            dve.scalar_tensor_tensor(v2[9], v2[0], 0.0, v2[6], ALU.max, ALU.add)
            dve.wait_ge(c_ea, 1)
            dve.drain()
            dve.scalar_tensor_tensor(by_t[8], by_t[9], -1.0,
                                     dts[:, 5, 0:SH].unsqueeze(1).to_broadcast([P, TT, SH]), ALU.mult,
                                     ALU.mult).then_inc(c_dtA, 1)
            ahead(GR0 - 1)
            dve.wait_ge(c_acol, 1)
            acol = dts[:, 10:12].rearrange("p a b -> p (a b)")
            dve.tensor_copy(acol[:, 0:2 * SH], bank[7][:, 0:2 * SH])
            dve.drain()
            dve.tensor_tensor(acol[:, 2 * SH:3 * SH], acol[:, 0:SH], bank[7][:, 2 * SH:3 * SH], ALU.subtract)
            dve.drain()
            for s in range(G + 3):
                if s < G:
                    ahead(GR0 + 2 * s + 2)
                    dve.wait_ge(c_u, 2 * s + 2)
                    if s >= 1:
                        dve.wait_ge(c_xc, 4 * s)
                    for tap in range(CONV):
                        for i, ct in enumerate((2 * s, 2 * s + 1, KI + s, KI + G + s)):
                            w = cwT[:, tap, ct:ct + 1]
                            if tap == 0:
                                ins = dve.tensor_scalar(acc[:, i], U[:, i, 0:T], w, None, ALU.mult)
                            else:
                                ins = dve.scalar_tensor_tensor(acc[:, i], U[:, i, tap:tap + T], w, acc[:, i],
                                                               ALU.mult, ALU.add)
                        if tap < CONV - 1:
                            dve.drain()
                    ins.then_inc(c_conv, 1)
                    ahead(GR0 + 2 * s + 3)
                g = s - 2
                if 0 <= g < G:
                    dve.wait_ge(c_y, g + 1)
                    yg_ = y[:, :, g * 256:(g + 1) * 256]
                    dve.tensor_tensor(yg_, yg_, bank[6][:].rearrange("p (t c) -> p t c", t=TT),
                                      ALU.add).then_inc(c_yadd, 1)
                g = s - 1
                if 0 <= g < G:
                    hs = slice(g * REP, (g + 1) * REP)
                    dve.wait_ge(c_abc, g + 1)
                    if g >= 1:
                        dve.wait_ge(c_m, g)
                    for b, (tile, off) in enumerate(((0, 0), (1, 2), (1, 1))):
                        for r in range(REP):
                            ins = dve.tensor_scalar(arg[:, b, r], bank[4 + tile][:, r * P:(r + 1) * P],
                                                    acol[:, off * SH + g * REP + r:off * SH + g * REP + r + 1], 0.0,
                                                    ALU.subtract, ALU.min)
                    ins.then_inc(c_arg, 1)
                    dve.wait_ge(c_xT, g + 1)
                    if g >= 1:
                        dve.wait_ge(c_y, g)
                    for t in range(TT):
                        xt = bank[2][:, t * T:(t + 1) * T].rearrange("p (r c) -> p r c", r=REP)
                        dve.tensor_tensor(Xdt[:, t].rearrange("p (r c) -> p r c", r=REP), xt,
                                          by_t[9][:, t, hs].unsqueeze(2).to_broadcast([P, REP, 64]), ALU.mult)
                        ins = dve.tensor_tensor(
                            y[:, t, g * 256:(g + 1) * 256].rearrange("p (r c) -> p r c", r=REP), xt,
                            dsk[:, hs].unsqueeze(2).to_broadcast([P, REP, 64]), ALU.mult)
                    ins.then_inc(c_xd, 1)
                    dve.wait_ge(c_cb, g + 1)
                    cb = bank[3][:, 0:3 * P].rearrange("p (b c) -> p b c", b=3)
                    dve.tensor_tensor(CBm[:, 0], cb[:, 0], tri[:], ALU.mult)
                    dve.tensor_copy(CBm[:, 1], cb[:, 1])
                    dve.tensor_tensor(CBm[:, 2], cb[:, 2], tri[:], ALU.mult).then_inc(c_xd, 1)
                    dve.drain()
                    dve.wait_ge(c_exp, g + 1)
                    for b in range(3):
                        ins = dve.tensor_tensor(M[:, b], arg[:, b], CBm[:, b].unsqueeze(1).to_broadcast([P, REP, P]),
                                                ALU.mult)
                    ins.then_inc(c_m, 1)
            dve.wait_ge(c_zs, 8)
            dve.drain()
            dve.tensor_tensor(y[:], y[:], z[:], ALU.mult).then_inc(c_gated, 1)
            dve.wait_ge(c_sq, 2)
            i = root(4, DI, st[:, 4], c_var, c_sqrt, 1, 1)
            for t in range(TT):
                dve.tensor_scalar(y[:, t], y[:, t], i[:, t:t + 1], None, ALU.mult).then_inc(c_yn, 1)

            def y_lo(i):
                dve.wait_ge(c_yThi, i + 1)
                part = (slice(None), slice(4 * (i % 4), 4 * (i % 4) + 4), slice((i // 4) * P, (i // 4 + 1) * P))
                dve.tensor_tensor(yT_lo[part], yT[:, i % 2].rearrange("p (a b) -> p a b", b=P),
                                  yT_hi[part].bitcast(F32), ALU.subtract).then_inc(c_yTsb, 1)

            for i in range(8):
                b = i % 4
                dve.wait_ge(c_yT, i + 1)
                if i >= 2:
                    dve.wait_ge(c_yTsb, i - 1)
                dve.tensor_tensor(yT[:, i % 2].rearrange("p (a b) -> p a b", b=P),
                                  bank[4 + b][:].rearrange("p (a b) -> p a b", b=P),
                                  vT[:, 32 + 4 * b:36 + 4 * b].unsqueeze(2).to_broadcast([P, 4, P]),
                                  ALU.mult).then_inc(c_yTg, 1)
                if i >= 1:
                    y_lo(i - 1)
            y_lo(7)
            ahead(MOE0 - 1)
            dve.wait_ge(chunk_used, SO0 + KI // 2)
            for t in range(TT):
                for i in range(2):
                    hh = h[:, t, 512 * i:512 * (i + 1)]
                    dve.tensor_tensor(hh, hh, bank[2 * t + i][:], ALU.add).then_inc(h_done, 1)
            norm(3, 24)
            for t in range(TT):
                dve.wait_ge(xs_his, t + 1)
                dve.tensor_tensor(xs_lo[:, t], xs[:, t], xs_hi[:, t].bitcast(F32), ALU.subtract).then_inc(xs_los, 1)
            r2 = [rt[:, i] for i in range(16)]
            r3 = [rt[:, i].rearrange("p (t e) -> p t e", t=TT) for i in range(16)]
            dve.wait_ge(r_logit, 1)
            dve.tensor_copy(r2[0], bank[0][:, 0:TT * E])
            dve.drain()
            dve.tensor_reduce(rt[:, 7, 0:TT], r3[0], AXX, ALU.max)
            c = [cmp8[:, i].rearrange("p t (e j) -> p t e j", e=E) for i in range(2)]
            lj = r3[0].unsqueeze(2).to_broadcast([P, TT, E, E])
            le = r3[0].unsqueeze(3).to_broadcast([P, TT, E, E])
            dve.tensor_tensor(c[0], lj, le, ALU.is_gt)
            dve.tensor_tensor(c[1], lj, le, ALU.is_equal)
            dve.drain()
            dve.tensor_tensor(c[1], c[1], jlt[:].unsqueeze(1).to_broadcast([P, TT, E, E]), ALU.mult)
            dve.drain()
            dve.tensor_tensor(c[0], c[0], c[1], ALU.add)
            dve.drain()
            dve.tensor_reduce(r3[3], c[0], AXX, ALU.add)
            dve.drain()
            dve.tensor_scalar(r2[5], r2[3], 1.5, None, ALU.is_lt).then_inc(r_sel, 1)
            dve.tensor_tensor(r3[1], r3[0], rt[:, 7, 0:TT].unsqueeze(2).to_broadcast([P, TT, E]),
                              ALU.subtract).then_inc(r_max, 1)
            dve.drain()
            dve.wait_ge(r_exp, 1)
            dve.tensor_tensor(r2[4], r2[2], r2[5], ALU.mult)
            dve.drain()
            dve.tensor_reduce(rt[:, 8, 0:TT], r3[4], AXX, ALU.add)
            dve.drain()
            dve.reciprocal(rt[:, 8, 0:TT], rt[:, 8, 0:TT])
            dve.drain()
            dve.memset(gate17[:], 0.0)
            dve.memset(place17[:], -1.0)
            dve.drain()
            for i in range(2):
                dve.tensor_tensor(gate17[:, :, i * E:(i + 1) * E], r3[4],
                                  rt[:, 8, 0:TT].unsqueeze(2).to_broadcast([P, TT, E]), ALU.mult)
            dve.wait_ge(r_cnt, 1)
            dve.tensor_scalar(r2[6], bank[1][:, 0:2 * E], 1.0, None, ALU.add)
            dve.tensor_reduce(rt[:, 9, 0:1], bank[1][:, 2 * E:3 * E], AXX, ALU.max)
            dve.drain()
            dve.tensor_tensor(r2[6], r2[6], r2[5], ALU.mult)
            dve.tensor_scalar(rt[:, 9, 1:2], rt[:, 9, 0:1], float(P), float(E), ALU.is_gt, ALU.mult)
            dve.drain()
            dve.tensor_scalar(place17[:, :, 0:E], r3[6], -1.0, None, ALU.add)
            dve.tensor_scalar(place17[:, :, E:2 * E], r3[6], -1.0 - P, None, ALU.add)
            dve.tensor_scalar(passes_i[:], rt[:, 9, 1:2], float(E), None, ALU.add).then_inc(r_passes, 1)
            dve.drain()
            dve.wait_ge(r_passes, 1)
            passes = dve.value_load(passes_i[0:1, 0:1], min_val=E, max_val=2 * E)

            for t in range(TT):
                ins = dve.tensor_scalar(sel[:, t], places[:], place17[:, t, 0:1], None, ALU.is_equal)
            ins.then_inc(m_S, 1)
            dve.sem_inc(m_h, 1)
            dve.memset(gselT, 0.0).then_inc(m_gtsb, 1)
            for i in range(2):
                dve.memset(yg[:, 512 * i:512 * (i + 1)], 0.0).then_inc(m_ysb, 1)
            dve.sem_inc(m_Tsb, 1)

            def gathered_lo(at):
                dve.wait_ge(m_xghi, at + 1)
                for k in range(KD):
                    ins = dve.scalar_tensor_tensor(xgT_lo[:, k], bank[6 + k // 4][:, (k % 4) * P:(k % 4 + 1) * P],
                                                   vT[:, 24 + k:25 + k], xgT_hi[:, k].bitcast(F32), ALU.mult,
                                                   ALU.subtract)
                ins.then_inc(m_xg, 1)

            gathered_lo(0)

            def ahead_e(at, a, b):
                for c in range(a, b):
                    dve.wait_ge(hi_ready, at * LAYER_CHUNKS + (MOE0 + c + 1))
                    dve.tensor_tensor(w_lo[:, c % SPLIT], ring[:, c % RING], w_hi[:, c % SPLIT].bitcast(F32),
                                      ALU.subtract).then_inc(lo_ready, 1)

            def add(at):
                for t in range(TT):
                    dve.wait_ge(m_comb, at * 2 + (t + 1))
                    for i in range(2):
                        hh = h[:, t, 512 * i:512 * (i + 1)]
                        ins = dve.tensor_tensor(hh, hh, bank[(6, 2)[t] + i][:], ALU.add)
                    ins.then_inc(m_add, 1)

            ahead_e(0, 0, AHEAD)
            with dve.Fori(0, passes) as it:

                def m_lo(j):
                    dve.wait_ge(m_This, it * NJ + (j + 1))
                    dve.tensor_tensor(m_hT_lo[:, 4 * j:4 * j + 4, :],
                                      bank[4 + j % 2][:].rearrange("p (a b) -> p a b", b=P),
                                      m_hT_hi[:, 4 * j:4 * j + 4, :].bitcast(F32), ALU.subtract).then_inc(m_Tsb, 1)

                ahead_e(it, AHEAD, 4)
                dve.wait_ge(m_gath, it * 2 + 2)
                for t in range(TT):
                    ins = dve.tensor_scalar(sel[:, t], places[:], place17[:, t, bass.ds(it + 1, 1)], None,
                                            ALU.is_equal)
                ins.then_inc(m_S, 1)
                dve.wait_ge(m_gt, it + 1)
                for t in range(TT):
                    ins = dve.tensor_scalar(gsel[:, t], places[:], place17[:, t, bass.ds(it, 1)],
                                            gate17[:, t, bass.ds(it, 1)], ALU.is_equal, ALU.mult)
                ins.then_inc(m_gs, 1)
                for j in range(NJ):
                    if j == 0:
                        add(it)
                    else:
                        ahead_e(it, 4 * j + 2, 4 * j + 4)
                        m_lo(j - 1)
                    ahead_e(it, 4 * j + 4, 4 * j + 6)
                    dve.wait_ge(chunk_used, it * LAYER_CHUNKS + (MOE0 + 4 * j + 4))
                    dve.wait_ge(m_silu, it * NJ + (1 + j + 1))
                    dve.wait_ge(m_T, it * NJ + (1 + j))
                    dve.tensor_tensor(m_hh[:, 0], m_sg[:, 0], bank[1][:], ALU.mult).then_inc(m_h, 1)
                ahead_e(it, 4 * NJ + 2, 4 * NJ + 3)
                gathered_lo(it + 1)
                ahead_e(it, 4 * NJ + 3, 6 * NJ - 1)
                m_lo(NJ - 1)
                ahead_e(it, 6 * NJ - 1, 6 * NJ)
                dve.wait_ge(m_gt, it + 2)
                dve.tensor_copy(gselT[:].rearrange("p a b -> p (a b)"), bank[0][:, 0:T]).then_inc(m_gtsb, 1)
                ahead_e(it + 1, 0, AHEAD)
            dve.drain()
            add(passes)
            dve.drain()
            for t in range(TT):
                dve.scalar_tensor_tensor(xs[:, t], h[:, t], 1.0, h[:, t], ALU.mult, ALU.mult,
                                         accum_out=st[:, 4, t:t + 1])
            dve.drain()
            i = root(4, D, st[:, 4], var_done, sqrt_done, 1, 5)
            dve.wait_ge(gain_loaded, 16)
            for t in range(TT):
                dve.scalar_tensor_tensor(xs[:, t], h[:, t], i[:, t:t + 1], gfin[:], ALU.mult,
                                         ALU.mult).then_inc(out_ready, 1)


_INS = ["x", "positions", "ln_mix", "ln_ffn", "ln_final", "swa_w_qkv", "swa_b_qkv", "swa_sinks", "swa_w_o",
        "ssm_w_in", "ssm_conv_w", "ssm_conv_b", "ssm_dt_bias", "ssm_a_log", "ssm_d", "ssm_norm", "ssm_w_out",
        "ffn_w_gu", "ffn_w_down", "moe_w_router", "moe_w_gu", "moe_w_down"]


def kernel(**inputs):
    import concourse.bacc as bacc
    from concourse.bass_utils import run_bass_kernel_spmd

    nc = bacc.Bacc("TRN2", target_bir_lowering=False, num_devices=1)
    arrays, args = {}, {}
    for name in _INS:
        a = np.ascontiguousarray(inputs[name])
        arrays[name + "_in"] = a
        args[name] = nc.dram_tensor(name + "_in", a.shape, mybir.dt.from_np(a.dtype), kind="ExternalInput").ap()
    args["out"] = nc.dram_tensor("out", (1, T, D), F32, kind="ExternalOutput").ap()
    build(nc, **args)
    got = run_bass_kernel_spmd(nc, [arrays], core_ids=[0])
    return got.results[0]["out"]
```

```python
import math
from contextlib import ExitStack

import numpy as np
import concourse.bass as bass
from concourse import mybir

ALU = mybir.AluOpType
ACT = mybir.ActivationFunctionType
F32 = mybir.dt.float32
F32R = mybir.dt.float32r
I32 = mybir.dt.int32
AXX = mybir.AxisListType.X

P = 128
T = 256
TT = T // P
D = 1024
KD = D // P
EPS = 1e-6
CH = 64
HEADS, KV, HD = 16, 2, 64
PAIRS = HEADS // 2
QKV = (HEADS + 2 * KV) * HD
ROT = HD // 4
NF = ROT // 2
THETA = 500000.0
FF = 3584
KF = FF // P
NJ = FF // 512
DI = 2 * D
KI = DI // P
G, REP, N = 8, 4, 128
SH = G * REP
CONV = 4
CT = (DI + 2 * G * N) // P
E = 8

RING = 6
SPLIT = 3
AHEAD = 2
SLOT = 2048
LAYER_CHUNKS = 6 * NJ


def build(nc, x, positions, ln_mix, ln_ffn, ln_final, swa_w_qkv, swa_b_qkv, swa_sinks, swa_w_o,
          ssm_w_in, ssm_conv_w, ssm_conv_b, ssm_dt_bias, ssm_a_log, ssm_d, ssm_norm, ssm_w_out,
          ffn_w_gu, ffn_w_down, moe_w_router, moe_w_gu, moe_w_down, out):
    ctx = ExitStack()

    def sb(name, shape, dt=F32):
        return ctx.enter_context(nc.sbuf_tensor(name, shape, dt))

    def sem(name):
        return ctx.enter_context(nc.semaphore(name))

    with ctx:
        def block_of(w, k0, k, a, n):
            return w.rearrange("(k p) n -> p k n", p=P)[:, k0:k0 + k, a:a + n]

        def halves(w, a, n):
            return [[(block_of(w, k0, 4, a, n), 4, 0, n)] for k0 in (0, 4)]

        B0, C0 = DI + DI, DI + DI + G * N
        stream = []
        for a, n in ((0, 512), (512, 512), (1024, 256)):
            stream += halves(swa_w_qkv[0], a, n)
        for a in (0, 512):
            stream += halves(swa_w_o[0], a, 512)
        for j in range(NJ):
            stream += halves(ffn_w_gu[0], j * 512, 512) + halves(ffn_w_gu[0], FF + j * 512, 512)
        for c in range(KF // 2):
            stream.append([(block_of(ffn_w_down[0], 2 * c, 2, 0, D), 2, 0, D)])
        for a in range(0, DI, 512):
            stream += halves(ssm_w_in[0], a, 512)
        for g in range(G):
            for k0 in (0, 4):
                stream.append([(block_of(ssm_w_in[0], k0, 4, DI + 256 * g, 256), 4, 0, 256),
                               (block_of(ssm_w_in[0], k0, 4, B0 + 128 * g, 128), 4, 256, 128),
                               (block_of(ssm_w_in[0], k0, 4, C0 + 128 * g, 128), 4, 384, 128)])
        for c in range(KI // 2):
            stream.append([(block_of(ssm_w_out[0], 2 * c, 2, 0, D), 2, 0, D)])
        QKV0, WO0, FGU0 = 0, 6, 10
        FDN0 = FGU0 + 4 * NJ
        Z0 = FDN0 + KF // 2
        GR0, SO0, MOE0 = Z0 + 8, Z0 + 8 + 2 * G, Z0 + 8 + 2 * G + KI // 2
        assert len(stream) == MOE0 and MOE0 % RING == 0 and LAYER_CHUNKS % RING == 0

        ring = sb("ring", [P, RING, SLOT])
        w_hi = sb("w_hi", [P, SPLIT, SLOT], F32R)
        w_lo = sb("w_lo", [P, SPLIT, SLOT], F32R)
        slot_loaded = [sem(f"slot_loaded{r}") for r in range(RING)]
        hi_ready = sem("hi_ready")
        lo_ready = sem("lo_ready")
        chunk_used = sem("chunk_used")

        def loads_until(n):
            return sum(16 * len(stream[m]) for m in range(n % RING, n + 1, RING))

        slot_base = [loads_until(MOE0 - RING + r) for r in range(RING)]

        def chunk(n, w):
            return tuple(v[:, n % SPLIT, 0:SLOT // w * w].rearrange("p (k n) -> p k n", n=w)
                         for v in (w_hi, w_lo))

        h = sb("h", [P, TT, D])
        xs = sb("xs", [P, TT, D])
        hT = sb("hT", [P, KD, T])
        hT_hi = sb("hT_hi", [P, KD, T], F32R)
        hT_lo = sb("hT_lo", [P, KD, T], F32R)
        ident = sb("ident", [P, P])
        tri = sb("tri", [P, P])
        tri_lt = sb("tri_lt", [P, P])
        ones = sb("ones", [P, P])
        places = sb("places", [P, P])
        jlt = sb("jlt", [P, E, E])
        xs_hi = hT_hi[:].rearrange("p k (a b) -> p (k a b)", a=TT).rearrange("p (t d) -> p t d", t=TT)
        xs_lo = hT_lo[:].rearrange("p k (a b) -> p (k a b)", a=TT).rearrange("p (t d) -> p t d", t=TT)
        invf = sb("invf", [P, NF])
        vT = sb("vT", [P, P])
        cwT = sb("cwT", [P, CONV, CT])
        sinks_in = sb("sinks_in", [P, HEADS])
        sinks = sb("sinks", [P, HEADS])
        dtb = sb("dtb", [P, SH])
        alog = sb("alog", [P, SH])
        dsk = sb("dsk", [P, SH])
        dtw = sb("dtw", [P, KD, SH])
        rw = sb("rw", [P, KD, E])
        pos_i = sb("pos_i", [P, TT], I32)
        st = sb("st", [P, 5, 8])
        trig = sb("trig", [P, 4, TT, 2 * NF])
        sm = sb("sm", [P, TT, 4, HEADS])
        dts = sb("dts", [P, 12, 2 * SH])
        rt = sb("rt", [P, 16, TT * E])
        acol = dts[:, 10:12].rearrange("p a b -> p (a b)")
        root_table = sb("root_table", [P, 5])
        place17 = sb("place17", [P, TT, 2 * E + 1])
        gate17 = sb("gate17", [P, TT, 2 * E + 1])
        passes_i = sb("passes_i", [P, 1], I32)

        def phase(**shapes):
            with ExitStack() as held:
                return [held.enter_context(nc.sbuf_tensor(name, [P, *s[0]], s[1]))[:] for name, s in shapes.items()]

        qkv, kd, qT, kT, vmid, prob, pT, oT_hi = phase(
            qkv=((TT, QKV), F32), kd=((TT, KV, 2, HD), F32), qT=((PAIRS, T), F32), kT=((KV, T), F32),
            vmid=((KV * HD,), F32), prob=((TT, HEADS, P), F32), pT=((HEADS, P), F32),
            oT_hi=((PAIRS, T), F32R))
        oT_lo, = phase(oT_lo=((PAIRS, T), F32R))
        brow = prob[:].rearrange("p a b c -> p (a b c)")[:, 0:QKV]
        rtmp = pT[:].rearrange("p a b -> p (a b)")[:, 0:4 * (HEADS + KV) * NF]
        vecs = pT[:, 8]
        cwr = pT[:, 9]
        f_hT_hi, f_hT_lo = phase(f_hT_hi=((KF, T), F32R), f_hT_lo=((KF, T), F32R))
        f_sg, f_hh = xs[:, 0].rearrange("p (t n) -> p t n", t=TT), xs[:, 1].rearrange("p (t n) -> p t n", t=TT)
        z, y, U, acc, Xdt, arg, M, CBm, sq_out = phase(
            z=((G, TT, 256), F32), y=((G, TT, 256), F32), U=((4, T + 3), F32), acc=((4, T), F32),
            Xdt=((TT, REP * 64), F32), arg=((3, REP, P), F32), M=((3, REP, P), F32), CBm=((3, P), F32),
            sq_out=((TT, 256), F32))
        XC = xs[:].rearrange("p t (a b) -> p (t a b)", b=T).rearrange("p (s a b) -> p s a b", s=2, b=T)
        yT_hi, yT_lo = phase(yT_hi=((KI, T), F32R), yT_lo=((KI, T), F32R))
        sq_sums = rt[:, 10].rearrange("p (t g) -> p t g", t=TT)
        m_sg, m_hh, m_hT_hi, m_hT_lo, xgT_hi, xgT_lo, sel, gsel, gselT, yg, gfin, cmp8 = phase(
            m_sg=((1, 512), F32), m_hh=((1, 512), F32), m_hT_hi=((KF, P), F32R), m_hT_lo=((KF, P), F32R),
            xgT_hi=((KD, P), F32R), xgT_lo=((KD, P), F32R), sel=((TT, P), F32R), gsel=((TT, P), F32),
            gselT=((TT, P), F32), yg=((D,), F32), gfin=((D,), F32), cmp8=((2, TT, E * E), F32))

        bank = [ctx.enter_context(nc.psum_tensor(f"bank{i}", [P, 512], F32)) for i in range(8)]

        def place_of(head):
            return (head % 2) * PAIRS + head // 2

        x_loaded, pos_loaded, vec_loaded, bc_loaded, bias_loaded, dtw_loaded = map(
            sem, ("x_loaded", "pos_loaded", "vec_loaded", "bc_loaded", "bias_loaded", "dtw_loaded"))
        const_ready, vec_T, vec_sb = map(sem, ("const_ready", "vec_T", "vec_sb"))
        sq_done, var_done, sqrt_done, xs_done, xT_mm, hT_done, h_done = map(
            sem, ("sq_done", "var_done", "sqrt_done", "xs_done", "xT_mm", "hT_done", "h_done"))
        angle_done, trig_done, qkv_mm, qkv_sb, rope_done, qkT_mm, qkT_sb, s_mm, sm_sub, sm_exp = map(
            sem, ("angle_done", "trig_done", "qkv_mm", "qkv_sb", "rope_done", "qkT_mm", "qkT_sb", "s_mm",
                  "sm_sub", "sm_exp"))
        p_ready, pT_mm, pT_sb, o_mm, o_sb, wo_mm = map(
            sem, ("p_ready", "pT_mm", "pT_sb", "o_mm", "o_sb", "wo_mm"))
        f_gate, f_up, f_silu, f_h, f_T, f_Tsb = map(
            sem, ("f_gate", "f_up", "f_silu", "f_h", "f_T", "f_Tsb"))
        c_dt, c_nabs, c_e, c_u1, c_ln, c_ea, c_dtA, c_acol, c_z, c_zs = map(
            sem, ("c_dt", "c_nabs", "c_e", "c_u1", "c_ln", "c_ea", "c_dtA", "c_acol", "c_z", "c_zs"))
        c_proj, c_u, c_pad, c_conv, c_xc, c_xT, c_cb, c_abc, c_xd, c_arg, c_exp, c_m, c_y, c_yadd = map(
            sem, ("c_proj", "c_u", "c_pad", "c_conv", "c_xc", "c_xT", "c_cb", "c_abc", "c_xd", "c_arg",
                  "c_exp", "c_m", "c_y", "c_yadd"))
        c_gated, c_sq, c_var, c_sqrt, c_yT, c_yTsb = map(
            sem, ("c_gated", "c_sq", "c_var", "c_sqrt", "c_yT", "c_yTsb"))
        r_logit, r_max, r_exp, r_sel, r_cnt, r_passes = map(
            sem, ("r_logit", "r_max", "r_exp", "r_sel", "r_cnt", "r_passes"))
        m_S, m_gath, m_xg, m_gs, m_gt, m_gtsb, m_silu, m_h, m_T, m_Tsb, m_y, m_ysb, m_comb, \
            m_add = map(sem, ("m_S", "m_gath", "m_xg", "m_gs", "m_gt", "m_gtsb", "m_silu",
                              "m_h", "m_T", "m_Tsb", "m_y", "m_ysb", "m_comb", "m_add"))
        out_ready, out_stored = map(sem, ("out_ready", "out_stored"))
        gain_loaded = sem("gain_loaded")
        xs_his, xs_los = map(sem, ("xs_his", "xs_los"))
        hT_his, hT_los, o_los, f_This, c_yThi, m_This, m_xghi = map(
            sem, ("hT_his", "hT_los", "o_los", "f_This", "c_yThi", "m_This", "m_xghi"))

        block = ctx.enter_context(nc.Block())

        @block.sync
        def _(sp):
            for a, src in ((0, ln_mix), (16, ln_ffn), (32, ssm_norm), (48, ssm_conv_b)):
                rows = src.rearrange("l (k p) -> (l k) p", p=P)
                sp.dma_start(vecs[a:a + rows.shape[0], :], rows).then_inc(vec_loaded, 16)
            sp.dma_start(cwr, ssm_conv_w[0].rearrange("j (k p) -> (j k) p", p=P)).then_inc(vec_loaded, 16)
            for t in range(TT):
                sp.dma_start(pos_i[:, t:t + 1], positions[0, t * P:(t + 1) * P].unsqueeze(1)
                             ).then_inc(pos_loaded, 16)
            for n, pieces in enumerate(stream):
                if n == 2:
                    sp.dma_start(brow[0:1, :], swa_b_qkv).then_inc(bias_loaded, 16)
                if n >= RING:
                    sp.wait_ge(lo_ready, n - RING + 1)
                for src, k, a, w in pieces:
                    width = sum(p[3] for p in pieces)
                    dst = ring[:, n % RING, 0:k * width].rearrange("p (k n) -> p k n", n=width)
                    sp.dma_start(dst[:, :, a:a + w], src).then_inc(slot_loaded[n % RING], 16)
            def experts_chunks(at, e, a, b):
                for c in range(a, b):
                    sp.wait_ge(lo_ready, at * LAYER_CHUNKS + (MOE0 + c - RING + 1))
                    if c < 4 * NJ:
                        src = block_of(moe_w_gu[0, e], (c % 2) * 4, 4, (c // 2 % 2) * FF + (c // 4) * 512, 512)
                    else:
                        src = block_of(moe_w_down[0, e], 2 * (c - 4 * NJ), 2, 0, D)
                    dst = ring[:, c % RING, :].rearrange("p (k n) -> p k n", n=512 if c < 4 * NJ else D)
                    sp.dma_start(dst, src).then_inc(slot_loaded[c % RING], 16)

            experts_chunks(0, 0, 0, RING)
            sp.wait_ge(r_passes, 1)
            passes = sp.value_load(passes_i[0:1, 0:1], min_val=E, max_val=2 * E)
            with sp.Fori(0, passes, E) as first:
                with sp.Fori(0, E - 1) as e:
                    experts_chunks(first + e, e, RING, LAYER_CHUNKS)
                    experts_chunks(first + e + 1, e + 1, 0, RING)
                experts_chunks(first + (E - 1), E - 1, RING, LAYER_CHUNKS)
                experts_chunks(first + E, 0, 0, RING)
            sp.wait_ge(out_ready, TT)
            sp.dma_start(out[0].rearrange("(t p) d -> p t d", p=P), xs[:]).then_inc(out_stored, 16)
            sp.wait_ge(out_stored, 16)

        @block.gpsimd
        def _(pool_e):
            pool_e.memset(ident[:], 0.0)
            pool_e.memset(tri[:], 1.0)
            pool_e.memset(tri_lt[:], 1.0)
            pool_e.memset(ones[:], 1.0)
            pool_e.memset(jlt[:], 1.0)
            for i in range(NF):
                pool_e.memset(invf[:, i:i + 1], float(np.float32(THETA ** (-2.0 * i / ROT))))
            pool_e.iota(places[:], [[1, P]], base=0, channel_multiplier=0,
                        allow_small_or_imprecise_dtypes=True)
            pool_e.drain()
            pool_e.affine_select(out=ident[:], in_=ident[:], compare_op=ALU.not_equal, fill=1.0, base=0,
                                 pattern=[[-1, P]], channel_multiplier=1)
            pool_e.affine_select(out=tri[:], in_=tri[:], compare_op=ALU.is_ge, fill=0.0, base=0,
                                 pattern=[[1, P]], channel_multiplier=-1)
            pool_e.affine_select(out=tri_lt[:], in_=tri_lt[:], compare_op=ALU.is_ge, fill=0.0, base=-1,
                                 pattern=[[1, P]], channel_multiplier=-1)
            pool_e.affine_select(out=jlt[:], in_=jlt[:], compare_op=ALU.is_ge, fill=0.0, base=-1,
                                 pattern=[[1, E], [-1, E]], channel_multiplier=0)
            pool_e.drain()
            pool_e.memset(root_table[:], 0.0).then_inc(const_ready, 1)
            for dst, src in ((sinks_in, swa_sinks), (dtb, ssm_dt_bias), (alog, ssm_a_log), (dsk, ssm_d)):
                pool_e.dma_start(dst[:], src[0].partition_broadcast(P)).then_inc(bc_loaded, 16)
            pool_e.dma_start(rw[:], moe_w_router[0].rearrange("(k p) e -> p k e", p=P)).then_inc(bc_loaded, 16)
            pool_e.dma_start(dtw[:], block_of(ssm_w_in[0], 0, KD, C0 + G * N, SH)).then_inc(dtw_loaded, 16)

        @block.scalar
        def _(act):
            act.dma_start(h[:], x[0].rearrange("(t p) d -> p t d", p=P)).then_inc(x_loaded, 16)

            def load_roots(q):
                act.activation(root_table[:, q:q + 1], ones[:, q:q + 1], ACT.Sqrt)

            def norm(q, ready, counts):
                load_roots(q)
                for t in range(TT):
                    act.wait_ge(ready, counts[t])
                    act.activation(xs[:, t, :], h[:, t, :], ACT.Square,
                                   accum_out=st[:, q, t:t + 1]).then_inc(sq_done, 1)
                act.wait_ge(var_done, q + 1)
                act.activation(st[:, q, 4:6], st[:, q, 2:4], ACT.Sqrt).then_inc(sqrt_done, 1)

            split = [0]

            def ahead(n):
                while split[0] <= min(n, MOE0 - 1):
                    m = split[0]
                    act.wait_ge(slot_loaded[m % RING], loads_until(m))
                    if m >= SPLIT:
                        act.wait_ge(chunk_used, m - SPLIT + 1)
                    w = sum(p[3] * p[1] for p in stream[m])
                    act.activation(w_hi[:, m % SPLIT, 0:w], ring[:, m % RING, 0:w], ACT.Copy).then_inc(hi_ready, 1)
                    split[0] += 1

            def norm_hi(q):
                for i in range(4):
                    act.wait_ge(hT_done, 4 * q + i + 1)
                    part = (slice(None), slice((i % 2) * 4, (i % 2) * 4 + 4), slice((i // 2) * P, (i // 2 + 1) * P))
                    act.activation(hT_hi[part], hT[part], ACT.Copy).then_inc(hT_his, 1)

            act.wait_ge(const_ready, 1)
            norm(0, x_loaded, (16, 16))
            ahead(1)
            act.wait_ge(angle_done, 1)
            act.activation(trig[:, 3], trig[:, 2], ACT.Sin).then_inc(trig_done, 1)
            norm_hi(0)
            for n, w in enumerate((512, 512, 256)):
                for t in range(TT):
                    ahead(QKV0 + 2 * n + 3)
                    act.wait_ge(*((qkv_mm, n + 1), (chunk_used, QKV0 + 2 * n + 2))[t])
                    act.activation(qkv[:, t, 512 * n:512 * n + w], bank[3 * t + n][:, 0:w],
                                   ACT.Copy).then_inc(qkv_sb, 1)
            for t in range(TT):
                for i in range(3):
                    act.wait_ge(qkT_mm, 3 * t + i + 1)
                    w = 4 if i < 2 else KV
                    dst = (qT[:, 4 * i:4 * i + 4, t * P:(t + 1) * P] if i < 2 else kT[:, :, t * P:(t + 1) * P])
                    act.activation(dst, bank[3 * t + i][:, 0:w * P].rearrange("p (a b) -> p a b", b=P),
                                   ACT.Copy).then_inc(qkT_sb, 1)
            for t in range(TT):
                act.wait_ge(sm_sub, t + 1)
                act.activation(prob[:, t], prob[:, t], ACT.Exp)
                act.activation(sm[:, t, 2], sm[:, t, 2], ACT.Exp).then_inc(sm_exp, 1)
            for t in range(TT):
                if t == 1:
                    act.wait_ge(o_mm, 1)
                for i in range(4):
                    act.wait_ge(pT_mm, 4 * t + i + 1)
                    act.activation(pT[:, 4 * i:4 * i + 4, :], bank[4 * t + i][:].rearrange("p (a b) -> p a b", b=P),
                                   ACT.Copy).then_inc(pT_sb, 1)
                act.wait_ge(o_mm, t + 1)
                for i in range(2):
                    act.activation(oT_hi[:, 4 * i:4 * i + 4, t * P:(t + 1) * P],
                                   bank[2 * t + i][:].rearrange("p (a b) -> p a b", b=P),
                                   ACT.Copy).then_inc(o_sb, 1)
            ahead(WO0 + 5)
            norm(1, h_done, (4, 4))
            ahead(FGU0 + 2)
            norm_hi(1)
            for j in range(NJ + 1):
                for b in range(TT):
                    if j < NJ:
                        ahead(FGU0 + 4 * j + 3)
                        act.wait_ge(*((f_gate, j + 1), (chunk_used, FGU0 + 4 * j + 2))[b])
                        if j >= 1:
                            act.wait_ge(f_h, 2 * (j - 1) + b + 1)
                        act.activation(f_sg[:, b], bank[b][:], ACT.Silu).then_inc(f_silu, 1)
                    else:
                        ahead(FDN0 + 1)
                if j >= 1:
                    for b in range(TT):
                        act.wait_ge(f_T, 2 * (j - 1) + b + 1)
                        act.activation(f_hT_hi[:, 4 * (j - 1):4 * j, b * P:(b + 1) * P],
                                       bank[4 + b][:].rearrange("p (a b) -> p a b", b=P),
                                       ACT.Copy).then_inc(f_This, 1)
            ahead(Z0)
            norm(2, h_done, (6, 8))
            ahead(Z0 + 2)
            norm_hi(2)
            act.wait_ge(bc_loaded, 5 * 16)
            act.activation(dts[:, 5, 0:SH], alog[:], ACT.Exp).then_inc(c_ea, 1)
            act.wait_ge(c_nabs, 1)
            act.activation(dts[:, 2], dts[:, 1], ACT.Exp).then_inc(c_e, 1)
            act.wait_ge(c_u1, 1)
            act.activation(dts[:, 4], dts[:, 3], ACT.Ln).then_inc(c_ln, 1)
            for n in range(4):
                for t in range(TT):
                    i = 2 * n + t
                    ahead(Z0 + 2 * n + 3)
                    act.wait_ge(*((c_z, n + 1), (chunk_used, Z0 + 2 * n + 2))[t])
                    act.activation(z[:, 2 * n:2 * n + 2, t], bank[i % 4][:].rearrange("p (g c) -> p g c", g=2),
                                   ACT.Silu).then_inc(c_zs, 1)
            act.wait_ge(c_pad, 1)
            ahead(GR0 + 2)
            for s in range(G + 3):
                tiles = (2 * s, 2 * s + 1, KI + s, KI + G + s)
                if s < G:
                    for i in range(2):
                        act.wait_ge(*((c_proj, s + 1), (chunk_used, GR0 + 2 * s + 2))[i])
                        if s >= 1:
                            act.wait_ge(c_xc, 4 * s)
                        for a in (2 * i, 2 * i + 1):
                            act.activation(acc[:, a], bank[i][:, (a % 2) * T:(a % 2 + 1) * T], ACT.Copy,
                                           scale=cwT[:, CONV - 1, tiles[a]:tiles[a] + 1])
                        if s >= 1:
                            act.wait_ge(c_conv, s)
                        act.activation(U[:, 2 * i:2 * i + 2, 3:], bank[i][:].rearrange("p (a b) -> p a b", b=T),
                                       ACT.Copy).then_inc(c_u, 1)
                    ahead(GR0 + 2 * s + (3 if s < G - 1 else 4))
                    act.wait_ge(c_conv, s + 1)
                    if s >= 2:
                        act.wait_ge(c_cb, s - 1)
                    for i, ct in enumerate(tiles):
                        act.activation(XC[:, s % 2, i], acc[:, i], ACT.Silu,
                                       bias=vT[:, 48 + ct:49 + ct]).then_inc(c_xc, 1)
                if s >= G:
                    ahead(SO0 + 2 * (s - G + 1))
                g = s - 1
                if 0 <= g < G:
                    act.wait_ge(c_arg, g + 1)
                    act.activation(arg[:, 0:2], arg[:, 0:2], ACT.Exp)
                    for r in range(REP):
                        ins = act.activation(arg[:, 2, r], bank[5][:, r * P:(r + 1) * P], ACT.Exp,
                                             bias=acol[:, 2 * SH + g * REP + r:2 * SH + g * REP + r + 1])
                    ins.then_inc(c_exp, 1)
                if s < G:
                    ahead(GR0 + 2 * s + 4)
                g = s - 3
                if g >= 0:
                    act.wait_ge(c_yT, g + 1)
                    for t in range(TT):
                        act.activation(sq_out[:, t], y[:, g, t], ACT.Square,
                                       accum_out=sq_sums[:, t, g:g + 1]).then_inc(c_sq, 1)
                    for k in range(2):
                        act.activation(yT_hi[:, 2 * g + k], bank[7][:, k * T:(k + 1) * T], ACT.Copy,
                                       scale=vT[:, 32 + 2 * g + k:33 + 2 * g + k]).then_inc(c_yThi, 1)
            ahead(MOE0 - 1)
            act.wait_ge(c_var, 1)
            act.activation(st[:, 4, 4:6], st[:, 4, 2:4], ACT.Sqrt).then_inc(c_sqrt, 1)

            def ahead_e(at, a, b):
                for c in range(a, min(b, LAYER_CHUNKS)):
                    act.wait_ge(slot_loaded[c % RING], at * (LAYER_CHUNKS // RING * 16)
                                + (slot_base[c % RING] + 16 * (c // RING + 1)))
                    act.wait_ge(chunk_used, at * LAYER_CHUNKS + (MOE0 + c - SPLIT + 1))
                    act.activation(w_hi[:, c % SPLIT], ring[:, c % RING], ACT.Copy).then_inc(hi_ready, 1)

            ahead_e(0, 0, AHEAD)
            norm(3, h_done, (10, 12))
            for t in range(TT):
                act.wait_ge(xs_done, 6 + t + 1)
                act.activation(xs_hi[:, t], xs[:, t], ACT.Copy).then_inc(xs_his, 1)
            act.dma_start(gfin, ln_final.partition_broadcast(P)).then_inc(gain_loaded, 16)
            act.wait_ge(r_max, 1)
            act.activation(rt[:, 2], rt[:, 1], ACT.Exp).then_inc(r_exp, 1)
            act.wait_ge(r_passes, 1)
            passes = act.value_load(passes_i[0:1, 0:1], min_val=E, max_val=2 * E)

            def gathered(at):
                for k in range(KD):
                    if k % 4 == 0:
                        act.wait_ge(m_gath, at * 2 + (k // 4 + 1))
                    ins = act.activation(xgT_hi[:, k], bank[6 + k // 4][:, (k % 4) * P:(k % 4 + 1) * P], ACT.Copy,
                                         scale=vT[:, 24 + k:25 + k])
                    if k % 4 == 3:
                        ins.then_inc(m_xghi, 1)

            gathered(0)
            act.sem_inc(m_silu, 1)

            with act.Fori(0, passes) as it:
                for j in range(NJ):
                    ahead_e(it, max(4 * j, AHEAD), 4 * j + 4)
                    act.wait_ge(chunk_used, it * LAYER_CHUNKS + (MOE0 + 4 * j + 2))
                    act.wait_ge(m_h, it * NJ + (1 + j))
                    act.activation(m_sg[:, 0], bank[0][:], ACT.Silu).then_inc(m_silu, 1)
                    if j >= 1:
                        act.wait_ge(m_T, it * NJ + (1 + j))
                        act.activation(m_hT_hi[:, 4 * (j - 1):4 * j, :],
                                       bank[4 + (j - 1) % 2][:].rearrange("p (a b) -> p a b", b=P),
                                       ACT.Copy).then_inc(m_This, 1)
                ahead_e(it, 4 * NJ, 4 * NJ + 3)
                gathered(it + 1)
                ahead_e(it, 4 * NJ + 3, 6 * NJ - 1)
                act.wait_ge(m_T, it * NJ + (1 + NJ))
                act.activation(m_hT_hi[:, KF - 4:KF, :], bank[4 + (NJ - 1) % 2][:].rearrange("p (a b) -> p a b", b=P),
                               ACT.Copy).then_inc(m_This, 1)
                ahead_e(it, 6 * NJ - 1, 6 * NJ)
                ahead_e(it + 1, 0, AHEAD)
                for i in range(2):
                    act.wait_ge(*((m_y, it + 1), (chunk_used, it * LAYER_CHUNKS + (MOE0 + LAYER_CHUNKS)))[i])
                    act.activation(yg[:, 512 * i:512 * (i + 1)], bank[2 + i][:], ACT.Copy).then_inc(m_ysb, 1)
            for r in range(AHEAD, RING):
                act.wait_ge(slot_loaded[r], passes * (LAYER_CHUNKS // RING * 16) + (slot_base[r] + 16))
            load_roots(4)
            act.wait_ge(var_done, 5)
            act.activation(st[:, 4, 4:6], st[:, 4, 2:4], ACT.Sqrt).then_inc(sqrt_done, 1)

        @block.tensor
        def _(pe):
            def product(o, stat, mov, start, stop):
                pe.matmul(o, stat[0], mov[0], start=start, stop=False)
                pe.matmul(o, stat[0], mov[1], start=False, stop=False)
                return pe.matmul(o, stat[1], mov[0], start=False, stop=stop)

            def part(pair, *at):
                return tuple(v[(slice(None), *at)] for v in pair)

            def have(n):
                pe.wait_ge(lo_ready, n + 1)

            hTs = (hT_hi, hT_lo)

            pe.wait_ge(const_ready, 1)
            pe.wait_ge(vec_loaded, 5 * 16)
            pe.transpose(bank[0][:, 0:80], vecs[0:80, :], ident[0:80, 0:80])
            pe.transpose(bank[0][:, P:2 * P], cwr[:], ident[:]).then_inc(vec_T, 1)

            def norm_T(q):
                for t in range(TT):
                    pe.wait_ge(xs_done, 2 * q + t + 1)
                    for k in range(KD):
                        ins = pe.transpose(bank[4 + 2 * t + k // 4][:, (k % 4) * P:(k % 4 + 1) * P],
                                           xs[:, t, k * P:(k + 1) * P], ident[:])
                        if k % 4 == 3:
                            ins.then_inc(xT_mm, 1)

            norm_T(0)
            pe.wait_ge(bias_loaded, 16)
            pe.wait_ge(vec_sb, 1)
            pe.wait_ge(hT_los, 4)
            for n, w in enumerate((512, 512, 256)):
                for t in range(TT):
                    pe.matmul(bank[3 * t + n][:, 0:w], ones[0:1, :], brow[0:1, 512 * n:512 * n + w],
                              start=True, stop=False)
                for half in range(2):
                    have(QKV0 + 2 * n + half)
                    wv = part(chunk(QKV0 + 2 * n + half, w), slice(0, 4))
                    for t in range(TT):
                        o = bank[3 * t + n][:, 0:w]
                        for k in range(4):
                            ins = product(o, part(hTs, 4 * half + k, slice(t * P, (t + 1) * P)), part(wv, k),
                                          False, half == 1 and k == 3)
                        if t == 1 or half == 1:
                            ins.then_inc((qkv_mm, chunk_used)[t], 1)
            for t in range(TT):
                pe.wait_ge(rope_done, t + 1)
                for i in range(3):
                    for a in range(4 if i < 2 else KV):
                        src = (qkv[:, t, (4 * i + a) * P:(4 * i + a + 1) * P] if i < 2 else
                               kd[:, t, a].rearrange("p a b -> p (a b)"))
                        ins = pe.transpose(bank[3 * t + i][:, a * P:(a + 1) * P], src, ident[:])
                    ins.then_inc(qkT_mm, 1)
            pe.wait_ge(qkT_sb, 6)
            for t in range(TT):
                for hd in range(HEADS):
                    s = place_of(hd)
                    r = slice((hd % 2) * HD, (hd % 2 + 1) * HD)
                    kv = hd // (HEADS // KV)
                    for c in (2 * t, 2 * t + 1):
                        half = c % 2
                        keys = {0: (0, 0), 1: (0, 1), 2: (2, 1), 3: (2, 3)}[c]
                        for i, kc in enumerate(keys):
                            ins = pe.matmul(
                                bank[4 * t + s // 4][half * CH:(half + 1) * CH,
                                                      (s % 4) * P + i * CH:(s % 4) * P + (i + 1) * CH],
                                qT[r, hd // 2, c * CH:(c + 1) * CH], kT[r, kv, kc * CH:(kc + 1) * CH],
                                start=True, stop=True)
                ins.then_inc(s_mm, 1)
            for t in range(TT):
                pe.wait_ge(p_ready, t + 1)
                for s in range(HEADS):
                    ins = pe.transpose(bank[4 * t + s // 4][:, (s % 4) * P:(s % 4 + 1) * P], prob[:, t, s],
                                       ident[:])
                    if s % 4 == 3:
                        ins.then_inc(pT_mm, 1)
                pe.wait_ge(pT_sb, 4 * (t + 1))
                for hd in range(HEADS):
                    kv = hd // (HEADS // KV)
                    for c in (2 * t, 2 * t + 1):
                        v = (vmid[:, kv * HD:(kv + 1) * HD] if c == 2 else
                             qkv[:, t, (HEADS + KV + kv) * HD:(HEADS + KV + kv + 1) * HD])
                        pair = hd // 2
                        ins = pe.matmul(bank[2 * t + pair // 4][(hd % 2) * HD:(hd % 2 + 1) * HD,
                                                               (pair % 4) * P + (c % 2) * CH:
                                                               (pair % 4) * P + (c % 2 + 1) * CH],
                                        v, pT[:, place_of(hd), (c % 2) * CH:(c % 2 + 1) * CH], start=True, stop=True)
                ins.then_inc(o_mm, 1)
            def times_1024(n, stat, outs, done):
                for half in range(2):
                    have(n + half)
                    wv = chunk(n + half, 512)
                    for t in range(TT):
                        for k in range(4):
                            ins = product(outs[t], part(stat, 4 * half + k, slice(t * P, (t + 1) * P)),
                                          part(wv, k), half == 0 and k == 0, half == 1 and k == 3)
                        if t == 1 or half == 1:
                            ins.then_inc((done, chunk_used)[t], 1)

            pe.wait_ge(o_los, 4)
            for n in range(2):
                times_1024(WO0 + 2 * n, (oT_hi, oT_lo), [bank[4 + 2 * n + t][:] for t in range(TT)], wo_mm)

            norm_T(1)
            pe.wait_ge(hT_los, 8)

            def f_transposes(j):
                for b in range(TT):
                    pe.wait_ge(f_h, 2 * j + b + 1)
                    if j >= 1:
                        pe.wait_ge(f_Tsb, 2 * (j - 1) + b + 1)
                    for a in range(4):
                        ins = pe.transpose(bank[4 + b][:, a * P:(a + 1) * P], f_hh[:, b, a * P:(a + 1) * P],
                                           ident[:])
                    ins.then_inc(f_T, 1)

            for j in range(NJ):
                for gu, done in ((0, f_gate), (1, f_up)):
                    if j >= 1:
                        pe.wait_ge((f_silu, f_h)[gu], 2 * j)
                    times_1024(FGU0 + 4 * j + 2 * gu, hTs, [bank[2 * gu + b][:] for b in range(TT)], done)
                    if gu == 0 and j >= 1:
                        f_transposes(j - 1)
            f_transposes(NJ - 1)

            def times_rows(n, stat, c, k_tiles, tiles=range(TT)):
                have(n + c)
                wv = chunk(n + c, D)
                for k in range(2):
                    for t in tiles:
                        for i in range(2):
                            ins = product(bank[2 * t + i][:], part(stat, 2 * c + k, slice(t * P, (t + 1) * P)),
                                          part(wv, k, slice(512 * i, 512 * (i + 1))), c == 0 and k == 0,
                                          c == k_tiles // 2 - 1 and k == 1)
                if tiles[-1] == TT - 1:
                    ins.then_inc(chunk_used, 1)

            for c in range(KF // 2):
                if c % 2 == 0:
                    pe.wait_ge(f_Tsb, 2 * (c // 2 + 1))
                times_rows(FDN0, (f_hT_hi, f_hT_lo), c, KF)

            norm_T(2)
            pe.wait_ge(hT_done, 12)
            pe.wait_ge(dtw_loaded, 16)
            for t in range(TT):
                for k in range(KD):
                    ins = pe.matmul(bank[6][:, t * SH:(t + 1) * SH], hT[:, k, t * P:(t + 1) * P], dtw[:, k, :],
                                    start=(k == 0), stop=(k == KD - 1))
            ins.then_inc(c_dt, 1)
            pe.wait_ge(hT_los, 12)
            for n in range(4):
                if n >= 2:
                    pe.wait_ge(c_zs, 2 * n - 2)
                times_1024(Z0 + 2 * n, hTs, [bank[(2 * n + t) % 4][:] for t in range(TT)], c_z)
            pe.wait_ge(c_dtA, 1)
            dtA = dts[:, 8].rearrange("p (t h) -> p t h", t=TT)
            pe.matmul(bank[7][:, 0:SH], tri[:], dtA[:, 0, :], start=True, stop=True)
            pe.matmul(bank[7][:, SH:2 * SH], tri[:], dtA[:, 1, :], start=True, stop=True)
            pe.matmul(bank[7][:, 2 * SH:3 * SH], ones[:], dtA[:, 0, :], start=True, stop=True).then_inc(c_acol, 1)
            pe.wait_ge(c_zs, 8)

            def y_transposes(g):
                pe.wait_ge(c_gated, g + 1)
                if g >= 1:
                    pe.wait_ge(c_yTsb, 2 * g)
                for k in range(2):
                    for t in range(TT):
                        ins = pe.transpose(bank[7][:, k * T + t * P:k * T + (t + 1) * P],
                                           y[:, g, t, k * P:(k + 1) * P], ident[:])
                ins.then_inc(c_yT, 1)

            def out_product(c, tiles=range(TT)):
                pe.wait_ge(c_yTsb, 2 * c + 2)
                times_rows(SO0, (yT_hi, yT_lo), c, KI, tiles)

            for s in range(G + 2):
                if s < G:
                    if s >= 1:
                        pe.wait_ge(c_u, 2 * s)
                    for half in range(2):
                        have(GR0 + 2 * s + half)
                        wv = chunk(GR0 + 2 * s + half, 512)
                        for i in range(4):
                            for k in range(4):
                                ins = product(bank[i // 2][:, (i % 2) * T:(i % 2 + 1) * T],
                                              part(wv, k, slice(i * P, (i + 1) * P)), part(hTs, 4 * half + k),
                                              half == 0 and k == 0 and i % 2 == 0,
                                              half == 1 and k == 3 and i % 2 == 1)
                            if i == 3 or (i == 1 and half == 1):
                                ins.then_inc((c_proj, chunk_used)[i // 2], 1)
                if s == G:
                    pe.wait_ge(c_u, 2 * G)
                    for c in range(3):
                        out_product(c, (0,))
                if s >= 3:
                    y_transposes(s - 3)
                g = s - 2
                if g >= 0:
                    pe.wait_ge(c_m, g + 1)
                    if g >= 1:
                        pe.wait_ge(c_yadd, g)
                    for r in range(REP):
                        xr = slice(r * 64, (r + 1) * 64)
                        pe.matmul(bank[6][:, r * 64:(r + 1) * 64], M[:, 0, r], Xdt[:, 0, xr],
                                  start=True, stop=True)
                        pe.matmul(bank[6][:, (REP + r) * 64:(REP + r + 1) * 64], M[:, 2, r], Xdt[:, 0, xr],
                                  start=True, stop=False)
                        ins = pe.matmul(bank[6][:, (REP + r) * 64:(REP + r + 1) * 64], M[:, 1, r],
                                        Xdt[:, 1, xr], start=False, stop=True)
                    ins.then_inc(c_y, 1)
                g = s - 1
                if 0 <= g < G:
                    if g >= 1:
                        pe.wait_ge(c_exp, g)
                    for t in range(TT):
                        for r in range(REP):
                            ins = pe.matmul(bank[4 + t][:, r * P:(r + 1) * P],
                                            dtA[:, t, g * REP + r:g * REP + r + 1].to_broadcast([P, P]), tri[:],
                                            start=True, stop=True)
                    ins.then_inc(c_abc, 1)
                    pe.wait_ge(c_xc, 4 * (g + 1))
                    if g >= 1:
                        pe.wait_ge(c_xd, 2 * g)
                    for t in range(TT):
                        for i in range(2):
                            ins = pe.transpose(bank[2][:, t * T + i * P:t * T + (i + 1) * P],
                                               XC[:, g % 2, i, t * P:(t + 1) * P], ident[:])
                    ins.then_inc(c_xT, 1)
                    B_, C_ = XC[:, g % 2, 2], XC[:, g % 2, 3]
                    pe.matmul(bank[3][:, 0:T], B_[:, 0:P], C_, start=True, stop=True)
                    pe.matmul(bank[3][:, T:T + P], B_[:, P:T], C_[:, P:T], start=True,
                              stop=True).then_inc(c_cb, 1)
                if s == G:
                    pe.wait_ge(c_xd, 2 * G)
                    for c in range(3):
                        out_product(c, (1,))
            for c in (3, 4):
                out_product(c)
            y_transposes(G - 1)
            for c in (5, 6, 7):
                out_product(c)

            norm_T(3)
            pe.wait_ge(hT_done, 16)
            pe.wait_ge(bc_loaded, 5 * 16)
            for t in range(TT):
                for k in range(KD):
                    ins = pe.matmul(bank[0][:, t * E:(t + 1) * E], hT[:, k, t * P:(t + 1) * P], rw[:, k, :],
                                    start=(k == 0), stop=(k == KD - 1))
            ins.then_inc(r_logit, 1)
            pe.wait_ge(r_sel, 1)
            chosen = rt[:, 5].rearrange("p (t e) -> p t e", t=TT)
            pe.matmul(bank[1][:, 0:E], tri_lt[:], chosen[:, 0, :], start=True, stop=True)
            pe.matmul(bank[1][:, E:2 * E], ones[:], chosen[:, 0, :], start=True, stop=False)
            pe.matmul(bank[1][:, E:2 * E], tri_lt[:], chosen[:, 1, :], start=False, stop=True)
            pe.matmul(bank[1][:, 2 * E:3 * E], ones[:], chosen[:, 0, :], start=True, stop=False)
            pe.matmul(bank[1][:, 2 * E:3 * E], ones[:], chosen[:, 1, :], start=False, stop=True).then_inc(r_cnt, 1)
            pe.wait_ge(r_passes, 1)
            passes = pe.value_load(passes_i[0:1, 0:1], min_val=E, max_val=2 * E)

            def gather(at):
                pe.wait_ge(m_S, at + 2)
                if not isinstance(at, int):
                    pe.wait_ge(m_add, at * 2 + 1)
                for k in range(KD):
                    for t in range(TT):
                        o = bank[6 + k // 4][:, (k % 4) * P:(k % 4 + 1) * P]
                        pe.matmul(o, xs_hi[:, t, k * P:(k + 1) * P], sel[:, t], start=(t == 0), stop=False)
                        ins = pe.matmul(o, xs_lo[:, t, k * P:(k + 1) * P], sel[:, t], start=False, stop=(t == 1))
                    if k % 4 == 3:
                        ins.then_inc(m_gath, 1)

            pe.sem_inc(m_T, 1)
            pe.sem_inc(m_gt, 1)
            pe.wait_ge(xs_los, TT)
            gather(-1)

            def combine(at):
                pe.wait_ge(m_gtsb, at + 1)
                pe.wait_ge(m_ysb, at * 2 + 2)
                for t in range(TT):
                    for i in range(2):
                        ins = pe.matmul(bank[(6, 2)[t] + i][:], gselT[:, t], yg[:, 512 * i:512 * (i + 1)],
                                        start=True, stop=True)
                    ins.then_inc(m_comb, 1)

            with pe.Fori(0, passes) as it:
                def have_e(c):
                    pe.wait_ge(lo_ready, it * LAYER_CHUNKS + (MOE0 + c + 1))

                def m_transposes(j):
                    pe.wait_ge(m_h, it * NJ + (1 + j + 1))
                    pe.wait_ge(m_Tsb, it * NJ + (1 + max(j - 1, 0)))
                    for a in range(4):
                        ins = pe.transpose(bank[4 + j % 2][:, a * P:(a + 1) * P], m_hh[:, 0, a * P:(a + 1) * P],
                                           ident[:])
                    ins.then_inc(m_T, 1)

                pe.wait_ge(m_xg, it + 1)
                for j in range(NJ):
                    for gu in range(2):
                        pe.wait_ge((m_silu, m_h)[gu], it * NJ + (1 + j))
                        if j == 0 and gu == 0:
                            pe.wait_ge(m_gtsb, it + 1)
                        for half in range(2):
                            c = 4 * j + 2 * gu + half
                            have_e(c)
                            wv = chunk(c, 512)
                            for k in range(4):
                                ins = product(bank[gu][:], part((xgT_hi, xgT_lo), 4 * half + k), part(wv, k),
                                              half == 0 and k == 0, half == 1 and k == 3)
                            ins.then_inc(chunk_used, 1)
                        if gu == 0:
                            m_transposes(j - 1) if j >= 1 else combine(it)
                gather(it)
                pe.wait_ge(m_add, it * 2 + 2)
                for c in range(2 * NJ):
                    if c == 2 * NJ - 2:
                        m_transposes(NJ - 1)
                        pe.wait_ge(m_gs, it + 1)
                        pe.wait_ge(m_silu, it * NJ + (1 + NJ))
                        for t in range(TT):
                            ins = pe.transpose(bank[0][:, t * P:(t + 1) * P], gsel[:, t], ident[:])
                        ins.then_inc(m_gt, 1)
                    have_e(4 * NJ + c)
                    wv = chunk(4 * NJ + c, D)
                    pe.wait_ge(m_Tsb, it * NJ + (1 + c // 2 + 1))
                    for k in range(2):
                        for i in range(2):
                            ins = product(bank[2 + i][:], part((m_hT_hi, m_hT_lo), 2 * c + k),
                                          part(wv, k, slice(512 * i, 512 * (i + 1))), c == 0 and k == 0,
                                          c == 2 * NJ - 1 and k == 1)
                            if c == 2 * NJ - 1 and k == 1 and i == 0:
                                ins.then_inc(m_y, 1)
                    ins.then_inc(chunk_used, 1)
            combine(passes)

        @block.vector
        def _(dve):
            def root(q, n, src, var, rooted, v_inc, rooted_at):
                s, v, r, i, u = (src[:, 2 * a:2 * a + 2] for a in (0, 1, 2, 3, 0))
                dve.tensor_scalar(v, s, 1.0 / n, EPS, ALU.mult, ALU.add).then_inc(var, v_inc)
                dve.wait_ge(rooted, rooted_at)
                dve.reciprocal(i, r)
                dve.drain()
                dve.tensor_tensor(u, i, i, ALU.mult)
                dve.drain()
                dve.tensor_tensor(u, u, v, ALU.mult)
                dve.drain()
                dve.tensor_scalar(u, u, -0.5, 1.5, ALU.mult, ALU.add)
                dve.drain()
                dve.tensor_tensor(i, i, u, ALU.mult)
                dve.drain()
                return i

            def norm(q, gain_at):
                dve.wait_ge(sq_done, 2 * q + 2)
                i = root(q, D, st[:, q], var_done, sqrt_done, 1, q + 1)
                for t in range(TT):
                    dve.tensor_scalar(xs[:, t, :], h[:, t, :], i[:, t:t + 1], None, ALU.mult).then_inc(xs_done, 1)
                for t in range(TT):
                    for k in (0, 4):
                        dve.wait_ge(xT_mm, 4 * q + 2 * t + k // 4 + 1)
                        dve.tensor_tensor(hT[:, k:k + 4, t * P:(t + 1) * P],
                                          bank[4 + 2 * t + k // 4][:].rearrange("p (a b) -> p a b", b=P),
                                          vT[:, gain_at + k:gain_at + k + 4].unsqueeze(2).to_broadcast([P, 4, P]),
                                          ALU.mult).then_inc(hT_done, 1)
                        if q < 3 and (t, k) != (0, 0):
                            norm_lo(q, 2 * t + k // 4 - 1)
                if q < 3:
                    norm_lo(q, 3)

            def norm_lo(q, i):
                dve.wait_ge(hT_his, 4 * q + i + 1)
                part = (slice(None), slice((i % 2) * 4, (i % 2) * 4 + 4), slice((i // 2) * P, (i // 2 + 1) * P))
                dve.tensor_tensor(hT_lo[part], hT[part], hT_hi[part].bitcast(F32), ALU.subtract).then_inc(hT_los, 1)

            split = [0]

            def ahead(n):
                while split[0] <= min(n, MOE0 - 1):
                    m = split[0]
                    dve.wait_ge(hi_ready, m + 1)
                    w = sum(p[3] * p[1] for p in stream[m])
                    dve.tensor_tensor(w_lo[:, m % SPLIT, 0:w], ring[:, m % RING, 0:w],
                                      w_hi[:, m % SPLIT, 0:w].bitcast(F32), ALU.subtract).then_inc(lo_ready, 1)
                    split[0] += 1

            dve.wait_ge(vec_T, 1)
            dve.tensor_copy(vT[:, 0:80], bank[0][:, 0:80])
            dve.tensor_copy(cwT[:].rearrange("p a b -> p (a b)"), bank[0][:, P:2 * P]).then_inc(vec_sb, 1)
            dve.wait_ge(pos_loaded, 32)
            dve.wait_ge(const_ready, 1)
            posf = rt[:, 0, 0:TT]
            dve.tensor_copy(posf, pos_i[:])
            dve.drain()
            for t in range(TT):
                for i in range(2):
                    dve.tensor_scalar(trig[:, 0, t, i * NF:(i + 1) * NF], invf[:], posf[:, t:t + 1], None, ALU.mult)
            dve.drain()
            for i, quarter in ((0, 0.0), (1, 0.25)):
                f = slice(i * NF, (i + 1) * NF)
                dve.tensor_scalar(trig[:, 1, :, f], trig[:, 0, :, f], 1.0 / (2 * math.pi), quarter, ALU.mult, ALU.add)
            dve.drain()
            dve.tensor_scalar(trig[:, 1], trig[:, 1], 12582912.0, None, ALU.add)
            dve.drain()
            dve.tensor_scalar(trig[:, 1], trig[:, 1], 12582912.0, None, ALU.subtract)
            dve.drain()
            left, src = 2 * math.pi, trig[:, 0]
            for bits in (5, 13, 21, 60):
                part = float(np.float32(left)) if bits == 60 else math.floor(left * 2.0 ** bits) / 2.0 ** bits
                left -= part
                dve.scalar_tensor_tensor(trig[:, 2], trig[:, 1], -part, src, ALU.mult, ALU.add)
                dve.drain()
                src = trig[:, 2]
            dve.tensor_scalar(trig[:, 2, :, NF:], trig[:, 2, :, NF:], math.pi / 2, None, ALU.add)
            dve.drain()
            dve.tensor_scalar(trig[:, 2], trig[:, 2], -3.1415925, 3.1415925, ALU.max, ALU.min).then_inc(angle_done, 1)

            norm(0, 0)
            ahead(QKV0 + 7)
            dve.wait_ge(trig_done, 1)
            tmp = rtmp.rearrange("p (a h f) -> p a h f", a=4, f=NF)
            for t in range(TT):
                dve.wait_ge(qkv_sb, 5 + t)
                heads = qkv[:, t, 0:(HEADS + KV) * HD].rearrange("p (h d) -> p h d", d=HD)
                t1, t2 = heads[:, :, 0:NF], heads[:, :, NF:2 * NF]
                sn = trig[:, 3, t, 0:NF].unsqueeze(1).to_broadcast([P, HEADS + KV, NF])
                cs = trig[:, 3, t, NF:].unsqueeze(1).to_broadcast([P, HEADS + KV, NF])
                for i, (a, b) in enumerate(((t1, cs), (t2, sn), (t2, cs), (t1, sn))):
                    dve.tensor_tensor(tmp[:, i], a, b, ALU.mult)
                dve.drain()
                dve.tensor_tensor(t1, tmp[:, 0], tmp[:, 1], ALU.subtract)
                dve.tensor_tensor(t2, tmp[:, 2], tmp[:, 3], ALU.add)
                dve.drain()
                for kv in range(KV):
                    ins = dve.tensor_copy(kd[:, t, kv], qkv[:, t, (HEADS + kv) * HD:(HEADS + kv + 1) * HD]
                                          .unsqueeze(1).to_broadcast([P, 2, HD]))
                src = qkv[(1 - t) * CH:(2 - t) * CH, t, (HEADS + KV) * HD:QKV]
                ins = dve.tensor_copy(vmid[(1 - t) * CH:(2 - t) * CH, :], src)
                ins.then_inc(rope_done, 1)
                dve.drain()
            scale = HD ** -0.5
            dve.wait_ge(bc_loaded, 5 * 16)
            dve.tensor_copy(sinks[:].rearrange("p (b a) -> p b a", b=2),
                            sinks_in[:].rearrange("p (a b) -> p b a", b=2))
            dve.drain()
            for t in range(TT):
                dve.wait_ge(s_mm, t + 1)
                for i in range(4):
                    dve.tensor_reduce(sm[:, t, 0, 4 * i:4 * i + 4],
                                      bank[4 * t + i][:].rearrange("p (a b) -> p a b", b=P), AXX, ALU.max)
                dve.drain()
                dve.scalar_tensor_tensor(sm[:, t, 1], sm[:, t, 0], scale, sinks[:], ALU.mult, ALU.max)
                dve.drain()
                dve.tensor_tensor(sm[:, t, 2], sinks[:], sm[:, t, 1], ALU.subtract)
                for i in range(4):
                    ins = dve.scalar_tensor_tensor(
                        prob[:, t, 4 * i:4 * i + 4], bank[4 * t + i][:].rearrange("p (a b) -> p a b", b=P), scale,
                        sm[:, t, 1, 4 * i:4 * i + 4].unsqueeze(2).to_broadcast([P, 4, P]), ALU.mult, ALU.subtract)
                ins.then_inc(sm_sub, 1)
                dve.wait_ge(sm_exp, t + 1)
                if t == 0:
                    dve.memset(prob[0:CH, 0, :, CH:], 0.0)
                    dve.drain()
                dve.tensor_reduce(sm[:, t, 3], prob[:, t], AXX, ALU.add)
                dve.drain()
                dve.tensor_tensor(sm[:, t, 3], sm[:, t, 3], sm[:, t, 2], ALU.add)
                dve.drain()
                dve.reciprocal(sm[:, t, 3], sm[:, t, 3])
                dve.drain()
                dve.tensor_tensor(prob[:, t], prob[:, t], sm[:, t, 3].unsqueeze(2).to_broadcast([P, HEADS, P]),
                                  ALU.mult).then_inc(p_ready, 1)
            for t in range(TT):
                for i in range(2):
                    dve.wait_ge(o_sb, 2 * t + i + 1)
                    part = (slice(None), slice(4 * i, 4 * i + 4), slice(t * P, (t + 1) * P))
                    dve.tensor_tensor(oT_lo[part], bank[2 * t + i][:].rearrange("p (a b) -> p a b", b=P),
                                      oT_hi[part].bitcast(F32), ALU.subtract).then_inc(o_los, 1)
            for n in range(2):
                ahead(WO0 + 2 * n + 3)
                for t in range(TT):
                    dve.wait_ge(*((wo_mm, n + 1), (chunk_used, WO0 + 2 * n + 2))[t])
                    hh = h[:, t, 512 * n:512 * (n + 1)]
                    dve.tensor_tensor(hh, hh, bank[4 + 2 * n + t][:], ALU.add).then_inc(h_done, 1)
            norm(1, 16)

            def f_lo(j):
                for b in range(TT):
                    dve.wait_ge(f_This, 2 * j + b + 1)
                    part = (slice(None), slice(4 * j, 4 * j + 4), slice(b * P, (b + 1) * P))
                    dve.tensor_tensor(f_hT_lo[part], bank[4 + b][:].rearrange("p (a b) -> p a b", b=P),
                                      f_hT_hi[part].bitcast(F32), ALU.subtract).then_inc(f_Tsb, 1)

            for j in range(NJ):
                ahead(FGU0 + 4 * j + 3)
                if j >= 1:
                    f_lo(j - 1)
                ahead(FGU0 + 4 * j + 5)
                for b in range(TT):
                    dve.wait_ge(*((f_up, j + 1), (chunk_used, FGU0 + 4 * j + 4))[b])
                    dve.wait_ge(f_silu, 2 * j + b + 1)
                    if j >= 1:
                        dve.wait_ge(f_T, 2 * (j - 1) + b + 1)
                    dve.tensor_tensor(f_hh[:, b], f_sg[:, b], bank[2 + b][:], ALU.mult).then_inc(f_h, 1)
            f_lo(NJ - 1)
            ahead(Z0)
            dve.wait_ge(chunk_used, FDN0 + KF // 2)
            for t in range(TT):
                for i in range(2):
                    hh = h[:, t, 512 * i:512 * (i + 1)]
                    dve.tensor_tensor(hh, hh, bank[2 * t + i][:], ALU.add).then_inc(h_done, 1)
            norm(2, 8)
            ahead(Z0 + 2)
            dve.memset(U[:, :, 0:3], 0.0).then_inc(c_pad, 1)
            dve.wait_ge(c_dt, 1)
            v2 = [dts[:, i] for i in range(12)]
            by_t = [dts[:, i].rearrange("p (t h) -> p t h", t=TT) for i in range(12)]
            dve.tensor_tensor(by_t[0], bank[6][:, 0:2 * SH].rearrange("p (t h) -> p t h", t=TT),
                              dtb[:].unsqueeze(1).to_broadcast([P, TT, SH]), ALU.add)
            dve.drain()
            dve.tensor_scalar(v2[1], v2[0], -1.0, None, ALU.mult)
            dve.drain()
            dve.tensor_tensor(v2[1], v2[1], v2[0], ALU.min).then_inc(c_nabs, 1)
            dve.wait_ge(c_e, 1)
            dve.tensor_scalar(v2[3], v2[2], 1.0, None, ALU.add).then_inc(c_u1, 1)
            dve.drain()
            dve.tensor_scalar(v2[6], v2[3], -1.0, None, ALU.add)
            dve.drain()
            dve.tensor_scalar(v2[7], v2[6], 0.0, None, ALU.is_equal)
            dve.drain()
            dve.tensor_tensor(v2[6], v2[6], v2[7], ALU.add)
            dve.drain()
            dve.reciprocal(v2[6], v2[6])
            dve.drain()
            dve.wait_ge(c_ln, 1)
            dve.tensor_tensor(v2[6], v2[6], v2[4], ALU.mult)
            dve.drain()
            dve.tensor_tensor(v2[6], v2[6], v2[7], ALU.add)
            dve.drain()
            dve.tensor_tensor(v2[6], v2[6], v2[2], ALU.mult)
            dve.drain()
            dve.scalar_tensor_tensor(v2[9], v2[0], 0.0, v2[6], ALU.max, ALU.add)
            dve.wait_ge(c_ea, 1)
            dve.drain()
            dve.scalar_tensor_tensor(by_t[8], by_t[9], -1.0,
                                     dts[:, 5, 0:SH].unsqueeze(1).to_broadcast([P, TT, SH]), ALU.mult,
                                     ALU.mult).then_inc(c_dtA, 1)
            ahead(GR0 + 1)
            dve.wait_ge(c_acol, 1)
            dve.tensor_copy(acol[:, 0:2 * SH], bank[7][:, 0:2 * SH])
            dve.drain()
            dve.tensor_tensor(acol[:, 2 * SH:3 * SH], bank[7][:, 2 * SH:3 * SH], acol[:, 0:SH], ALU.subtract)
            dve.drain()
            dve.wait_ge(c_zs, 8)
            ahead(GR0 + 2)
            for s in range(G + 3):
                if s < G:
                    dve.wait_ge(c_u, 2 * s + 2)
                    for tap in range(CONV - 1):
                        for i, ct in enumerate((2 * s, 2 * s + 1, KI + s, KI + G + s)):
                            ins = dve.scalar_tensor_tensor(acc[:, i], U[:, i, tap:tap + T], cwT[:, tap, ct:ct + 1],
                                                           acc[:, i], ALU.mult, ALU.add)
                        if tap < CONV - 2:
                            dve.drain()
                    ins.then_inc(c_conv, 1)
                    ahead(GR0 + 2 * s + (3 if s < G - 1 else 4))
                if s >= G:
                    ahead(SO0 + 2 * (s - G + 1))
                g = s - 2
                if 0 <= g < G:
                    dve.wait_ge(c_y, g + 1)
                    dve.tensor_tensor(y[:, g], y[:, g], bank[6][:].rearrange("p (t c) -> p t c", t=TT),
                                      ALU.add).then_inc(c_yadd, 1)
                    dve.drain()
                    dve.tensor_tensor(y[:, g], y[:, g], z[:, g], ALU.mult).then_inc(c_gated, 1)
                g = s - 1
                if 0 <= g < G:
                    hs = slice(g * REP, (g + 1) * REP)
                    dve.wait_ge(c_abc, g + 1)
                    if g >= 1:
                        dve.wait_ge(c_m, g)
                    for t in range(TT):
                        for r in range(REP):
                            ins = dve.tensor_scalar(arg[:, t, r], bank[4 + t][:, r * P:(r + 1) * P],
                                                    acol[:, t * SH + g * REP + r:t * SH + g * REP + r + 1], 0.0,
                                                    ALU.subtract, ALU.min)
                    ins.then_inc(c_arg, 1)
                    dve.wait_ge(c_xT, g + 1)
                    if g >= 1:
                        dve.wait_ge(c_y, g)
                    for t in range(TT):
                        xt = bank[2][:, t * T:(t + 1) * T].rearrange("p (r c) -> p r c", r=REP)
                        dve.tensor_tensor(Xdt[:, t].rearrange("p (r c) -> p r c", r=REP), xt,
                                          by_t[9][:, t, hs].unsqueeze(2).to_broadcast([P, REP, 64]), ALU.mult)
                        ins = dve.tensor_tensor(
                            y[:, g, t].rearrange("p (r c) -> p r c", r=REP), xt,
                            dsk[:, hs].unsqueeze(2).to_broadcast([P, REP, 64]), ALU.mult)
                    ins.then_inc(c_xd, 1)
                    dve.wait_ge(c_cb, g + 1)
                    cb = bank[3][:, 0:3 * P].rearrange("p (b c) -> p b c", b=3)
                    for t in range(TT):
                        dve.tensor_tensor(CBm[:, t], cb[:, 2 * t], tri[:], ALU.mult)
                    dve.tensor_copy(CBm[:, 2], cb[:, 1]).then_inc(c_xd, 1)
                    dve.drain()
                    dve.wait_ge(c_exp, g + 1)
                    dve.tensor_tensor(M[:], arg[:], CBm[:].unsqueeze(2).to_broadcast([P, 3, REP, P]),
                                      ALU.mult).then_inc(c_m, 1)
                if s < G:
                    ahead(GR0 + 2 * s + 4)
                g = s - 3
                if g >= 0:
                    dve.wait_ge(c_sq, 2 * (g + 1))
                    dve.wait_ge(c_yThi, 2 * g + 2)
                    for k in range(2):
                        dve.scalar_tensor_tensor(yT_lo[:, 2 * g + k], bank[7][:, k * T:(k + 1) * T],
                                                 vT[:, 32 + 2 * g + k:33 + 2 * g + k],
                                                 yT_hi[:, 2 * g + k].bitcast(F32), ALU.mult,
                                                 ALU.subtract).then_inc(c_yTsb, 1)
            ahead(MOE0 - 1)
            dve.tensor_reduce(st[:, 4, 0:2], sq_sums, AXX, ALU.add)
            dve.drain()
            i = root(4, DI, st[:, 4], c_var, c_sqrt, 1, 1)

            def ahead_e(at, a, b):
                for c in range(a, b):
                    dve.wait_ge(hi_ready, at * LAYER_CHUNKS + (MOE0 + c + 1))
                    dve.tensor_tensor(w_lo[:, c % SPLIT], ring[:, c % RING], w_hi[:, c % SPLIT].bitcast(F32),
                                      ALU.subtract).then_inc(lo_ready, 1)

            ahead_e(0, 0, AHEAD)
            dve.wait_ge(chunk_used, SO0 + KI // 2)
            for t in range(TT):
                for n in range(2):
                    hh = h[:, t, 512 * n:512 * (n + 1)]
                    dve.scalar_tensor_tensor(hh, bank[2 * t + n][:], i[:, t:t + 1], hh, ALU.mult,
                                             ALU.add).then_inc(h_done, 1)
            norm(3, 24)
            for t in range(TT):
                dve.wait_ge(xs_his, t + 1)
                dve.tensor_tensor(xs_lo[:, t], xs[:, t], xs_hi[:, t].bitcast(F32), ALU.subtract).then_inc(xs_los, 1)
            r2 = [rt[:, i] for i in range(16)]
            r3 = [rt[:, i].rearrange("p (t e) -> p t e", t=TT) for i in range(16)]
            dve.wait_ge(r_logit, 1)
            dve.tensor_copy(r2[0], bank[0][:, 0:TT * E])
            dve.drain()
            dve.tensor_reduce(rt[:, 7, 0:TT], r3[0], AXX, ALU.max)
            c = [cmp8[:, i].rearrange("p t (e j) -> p t e j", e=E) for i in range(2)]
            lj = r3[0].unsqueeze(2).to_broadcast([P, TT, E, E])
            le = r3[0].unsqueeze(3).to_broadcast([P, TT, E, E])
            dve.tensor_tensor(c[0], lj, le, ALU.is_gt)
            dve.tensor_tensor(c[1], lj, le, ALU.is_equal)
            dve.drain()
            dve.tensor_tensor(c[1], c[1], jlt[:].unsqueeze(1).to_broadcast([P, TT, E, E]), ALU.mult)
            dve.drain()
            dve.tensor_tensor(c[0], c[0], c[1], ALU.add)
            dve.drain()
            dve.tensor_reduce(r3[3], c[0], AXX, ALU.add)
            dve.drain()
            dve.tensor_scalar(r2[5], r2[3], 1.5, None, ALU.is_lt).then_inc(r_sel, 1)
            dve.tensor_tensor(r3[1], r3[0], rt[:, 7, 0:TT].unsqueeze(2).to_broadcast([P, TT, E]),
                              ALU.subtract).then_inc(r_max, 1)
            dve.drain()
            dve.wait_ge(r_exp, 1)
            dve.tensor_tensor(r2[4], r2[2], r2[5], ALU.mult)
            dve.drain()
            dve.tensor_reduce(rt[:, 8, 0:TT], r3[4], AXX, ALU.add)
            dve.drain()
            dve.reciprocal(rt[:, 8, 0:TT], rt[:, 8, 0:TT])
            dve.drain()
            dve.memset(gate17[:], 0.0)
            dve.memset(place17[:], -1.0)
            dve.drain()
            for i in range(2):
                dve.tensor_tensor(gate17[:, :, i * E:(i + 1) * E], r3[4],
                                  rt[:, 8, 0:TT].unsqueeze(2).to_broadcast([P, TT, E]), ALU.mult)
            dve.wait_ge(r_cnt, 1)
            dve.tensor_scalar(r2[6], bank[1][:, 0:2 * E], 1.0, None, ALU.add)
            dve.tensor_reduce(rt[:, 9, 0:1], bank[1][:, 2 * E:3 * E], AXX, ALU.max)
            dve.drain()
            dve.tensor_tensor(r2[6], r2[6], r2[5], ALU.mult)
            dve.tensor_scalar(rt[:, 9, 1:2], rt[:, 9, 0:1], float(P), float(E), ALU.is_gt, ALU.mult)
            dve.drain()
            dve.tensor_scalar(place17[:, :, 0:E], r3[6], -1.0, None, ALU.add)
            dve.tensor_scalar(place17[:, :, E:2 * E], r3[6], -1.0 - P, None, ALU.add)
            dve.tensor_scalar(passes_i[:], rt[:, 9, 1:2], float(E), None, ALU.add).then_inc(r_passes, 1)
            dve.drain()
            dve.wait_ge(r_passes, 1)
            passes = dve.value_load(passes_i[0:1, 0:1], min_val=E, max_val=2 * E)

            for t in range(TT):
                ins = dve.tensor_scalar(sel[:, t], places[:], place17[:, t, 0:1], None, ALU.is_equal)
            ins.then_inc(m_S, 1)
            dve.sem_inc(m_h, 1)
            dve.memset(gselT, 0.0).then_inc(m_gtsb, 1)
            for i in range(2):
                dve.memset(yg[:, 512 * i:512 * (i + 1)], 0.0).then_inc(m_ysb, 1)
            dve.sem_inc(m_Tsb, 1)

            def gathered_lo(at):
                for k in range(KD):
                    if k % 4 == 0:
                        dve.wait_ge(m_xghi, at * 2 + (k // 4 + 1))
                    ins = dve.scalar_tensor_tensor(xgT_lo[:, k], bank[6 + k // 4][:, (k % 4) * P:(k % 4 + 1) * P],
                                                   vT[:, 24 + k:25 + k], xgT_hi[:, k].bitcast(F32), ALU.mult,
                                                   ALU.subtract)
                ins.then_inc(m_xg, 1)

            gathered_lo(0)

            def add(at):
                for t in range(TT):
                    dve.wait_ge(m_comb, at * 2 + (t + 1))
                    for i in range(2):
                        hh = h[:, t, 512 * i:512 * (i + 1)]
                        ins = dve.tensor_tensor(hh, hh, bank[(6, 2)[t] + i][:], ALU.add)
                    ins.then_inc(m_add, 1)

            with dve.Fori(0, passes) as it:

                def m_lo(j):
                    dve.wait_ge(m_This, it * NJ + (j + 1))
                    dve.tensor_tensor(m_hT_lo[:, 4 * j:4 * j + 4, :],
                                      bank[4 + j % 2][:].rearrange("p (a b) -> p a b", b=P),
                                      m_hT_hi[:, 4 * j:4 * j + 4, :].bitcast(F32), ALU.subtract).then_inc(m_Tsb, 1)

                ahead_e(it, AHEAD, 4)
                dve.wait_ge(m_gath, it * 2 + 2)
                for t in range(TT):
                    ins = dve.tensor_scalar(sel[:, t], places[:], place17[:, t, bass.ds(it + 1, 1)], None,
                                            ALU.is_equal)
                ins.then_inc(m_S, 1)
                dve.wait_ge(m_gt, it + 1)
                for t in range(TT):
                    ins = dve.tensor_scalar(gsel[:, t], places[:], place17[:, t, bass.ds(it, 1)],
                                            gate17[:, t, bass.ds(it, 1)], ALU.is_equal, ALU.mult)
                ins.then_inc(m_gs, 1)
                for j in range(NJ):
                    if j == 0:
                        add(it)
                    else:
                        ahead_e(it, 4 * j + 2, 4 * j + 4)
                        m_lo(j - 1)
                    ahead_e(it, 4 * j + 4, 4 * j + 6)
                    dve.wait_ge(chunk_used, it * LAYER_CHUNKS + (MOE0 + 4 * j + 4))
                    dve.wait_ge(m_silu, it * NJ + (1 + j + 1))
                    dve.wait_ge(m_T, it * NJ + (1 + j))
                    dve.tensor_tensor(m_hh[:, 0], m_sg[:, 0], bank[1][:], ALU.mult).then_inc(m_h, 1)
                ahead_e(it, 4 * NJ + 2, 4 * NJ + 3)
                gathered_lo(it + 1)
                ahead_e(it, 4 * NJ + 3, 6 * NJ - 1)
                m_lo(NJ - 1)
                ahead_e(it, 6 * NJ - 1, 6 * NJ)
                dve.wait_ge(m_gt, it + 2)
                dve.tensor_copy(gselT[:].rearrange("p a b -> p (a b)"), bank[0][:, 0:T]).then_inc(m_gtsb, 1)
                ahead_e(it + 1, 0, AHEAD)
            dve.drain()
            add(passes)
            dve.drain()
            for t in range(TT):
                dve.scalar_tensor_tensor(xs[:, t], h[:, t], 1.0, h[:, t], ALU.mult, ALU.mult,
                                         accum_out=st[:, 4, t:t + 1])
            dve.drain()
            i = root(4, D, st[:, 4], var_done, sqrt_done, 1, 5)
            dve.wait_ge(gain_loaded, 16)
            for t in range(TT):
                dve.scalar_tensor_tensor(xs[:, t], h[:, t], i[:, t:t + 1], gfin[:], ALU.mult,
                                         ALU.mult).then_inc(out_ready, 1)


_INS = ["x", "positions", "ln_mix", "ln_ffn", "ln_final", "swa_w_qkv", "swa_b_qkv", "swa_sinks", "swa_w_o",
        "ssm_w_in", "ssm_conv_w", "ssm_conv_b", "ssm_dt_bias", "ssm_a_log", "ssm_d", "ssm_norm", "ssm_w_out",
        "ffn_w_gu", "ffn_w_down", "moe_w_router", "moe_w_gu", "moe_w_down"]


def kernel(**inputs):
    import concourse.bacc as bacc
    from concourse.bass_utils import run_bass_kernel_spmd

    nc = bacc.Bacc("TRN2", target_bir_lowering=False, num_devices=1)
    arrays, args = {}, {}
    for name in _INS:
        a = np.ascontiguousarray(inputs[name])
        arrays[name + "_in"] = a
        args[name] = nc.dram_tensor(name + "_in", a.shape, mybir.dt.from_np(a.dtype), kind="ExternalInput").ap()
    args["out"] = nc.dram_tensor("out", (1, T, D), F32, kind="ExternalOutput").ap()
    build(nc, **args)
    got = run_bass_kernel_spmd(nc, [arrays], core_ids=[0])
    return got.results[0]["out"]
```
